# Optimizing a Trainium2 kernel written in Bass

```python
import jax, jax.numpy as jnp
from jax import lax
import numpy as np

D_MODEL = 1024
BATCH = 1
SEQ = 256
DEPTH = 2

HEAD_DIM = 64
A_HEADS = 8
A_KV_RANK = 128
IDX_HEADS = 4
IDX_DIM = 64
IDX_TOPK_MAX = 256
B_HEADS = 8
C_HEADS = 16
MOBA_BLOCK = 256
MOBA_TOPK = 3
Q_BLOCK = 128
D_FF = -(-8 * D_MODEL // (3 * 256)) * 256
DEEPNORM_ALPHA = (2 * DEPTH) ** 0.25
DEEPNORM_BETA = (8 * DEPTH) ** -0.25
EVEN_IN = A_HEADS * HEAD_DIM + A_KV_RANK + IDX_HEADS * IDX_DIM + IDX_DIM + IDX_HEADS + 3 * B_HEADS * HEAD_DIM
ODD_IN = 3 * C_HEADS * HEAD_DIM
NEG = -1e30

kernel_name = "hybrid_dsa_stickbreak_moba_deepnorm"

def layer_norm(x, g, b, eps=1e-5):
    xf = x.astype(jnp.float32)
    mu = xf.mean(-1, keepdims=True)
    var = jnp.square(xf - mu).mean(-1, keepdims=True)
    return ((xf - mu) * lax.rsqrt(var + eps) * g.astype(jnp.float32) + b.astype(jnp.float32)).astype(x.dtype)

def rms_norm(x, g, eps=1e-6):
    xf = x.astype(jnp.float32)
    return (xf * lax.rsqrt(jnp.mean(xf * xf, -1, keepdims=True) + eps) * g.astype(jnp.float32)).astype(x.dtype)

def alibi_slopes(n):
    return jnp.asarray(2.0 ** (-8.0 * np.arange(1, n + 1) / n), dtype=jnp.float32)

def to_qblocks(t):
    B, S = t.shape[:2]
    return t.reshape((B, S // Q_BLOCK, Q_BLOCK) + t.shape[2:]).swapaxes(0, 1)

def from_qblocks(t):
    t = t.swapaxes(0, 1)
    return t.reshape((t.shape[0], t.shape[1] * t.shape[2]) + t.shape[3:])

def dsa_attention(q, c_kv, q_idx, k_idx, w_idx, w_uk, w_uv):
    B, S = q.shape[:2]
    topk = min(IDX_TOPK_MAX, S // 4)
    nq = S // Q_BLOCK
    slopes = alibi_slopes(A_HEADS)
    key_pos = jnp.arange(S)
    q_lat = jnp.einsum('bshd,hdr->bshr', q, w_uk)

    def block(args):
        qb, qib, wb, t0 = args
        tq = t0 + jnp.arange(Q_BLOCK)
        causal = key_pos[None, :] <= tq[:, None]
        dots = jnp.einsum('bqhd,bsd->bqhs', qib, k_idx).astype(jnp.float32) * IDX_DIM ** -0.5
        index = jnp.einsum('bqh,bqhs->bqs', wb.astype(jnp.float32), jax.nn.relu(dots))
        index = jnp.where(causal[None], index, NEG)
        _, sel = lax.top_k(index, topk)
        c_sel = jax.vmap(lambda c, i: c[i])(c_kv, sel)
        valid = sel <= tq[None, :, None]
        dist = (tq[None, :, None] - sel).astype(jnp.float32)
        logits = jnp.einsum('bqhr,bqkr->bqhk', qb, c_sel).astype(jnp.float32) * HEAD_DIM ** -0.5
        logits = logits - slopes[None, None, :, None] * dist[:, :, None, :]
        logits = jnp.where(valid[:, :, None, :], logits, NEG)
        p = jax.nn.softmax(logits, axis=-1).astype(c_sel.dtype)
        o_lat = jnp.einsum('bqhk,bqkr->bqhr', p, c_sel)
        return jnp.einsum('bqhr,hrd->bqhd', o_lat, w_uv)

    out = lax.map(block, (to_qblocks(q_lat), to_qblocks(q_idx), to_qblocks(w_idx),
                          jnp.arange(nq, dtype=jnp.int32) * Q_BLOCK))
    return from_qblocks(out)

def stick_breaking_attention(q, k, v):
    B, S = q.shape[:2]
    nq = S // Q_BLOCK
    key_pos = jnp.arange(S)

    def block(args):
        qb, t0 = args
        tq = t0 + jnp.arange(Q_BLOCK)
        strict = (key_pos[None, :] < tq[:, None])[None, None]
        z = jnp.einsum('bqhd,bshd->bhqs', qb, k).astype(jnp.float32) * HEAD_DIM ** -0.5
        log_beta = jax.nn.log_sigmoid(z)
        log_1m = jnp.where(strict, jax.nn.log_sigmoid(-z), 0.0)
        log_rem = lax.cumsum(log_1m, axis=3, reverse=True) - log_1m
        a = jnp.where(strict, jnp.exp(log_beta + log_rem), 0.0)
        return jnp.einsum('bhqs,bshd->bqhd', a.astype(v.dtype), v)

    out = lax.map(block, (to_qblocks(q), jnp.arange(nq, dtype=jnp.int32) * Q_BLOCK))
    return from_qblocks(out)

def moba_attention(q, k, v):
    B, S, H, D = q.shape
    P = MOBA_BLOCK
    nb = -(-S // P)
    kk = min(MOBA_TOPK, nb)
    pad = nb * P - S
    kp = jnp.pad(k, ((0, 0), (0, pad), (0, 0), (0, 0)))
    vp = jnp.pad(v, ((0, 0), (0, pad), (0, 0), (0, 0)))
    k_blk = kp.reshape(B, nb, P, H, D).transpose(0, 3, 1, 2, 4)
    v_blk = vp.reshape(B, nb, P, H, D).transpose(0, 3, 1, 2, 4)
    k_mean = k_blk.astype(jnp.float32).mean(axis=3)
    slopes = alibi_slopes(H)
    nq = S // Q_BLOCK
    q_chunks = q.reshape(B * nq, Q_BLOCK, H, D)
    b_ids = jnp.repeat(jnp.arange(B, dtype=jnp.int32), nq)
    t0s = jnp.tile(jnp.arange(nq, dtype=jnp.int32) * Q_BLOCK, B)
    hidx = jnp.arange(H)[None, :, None]
    blk_off = jnp.arange(P)

    def block(args):
        qb, b, t0 = args
        kb, vb, km = k_blk[b], v_blk[b], k_mean[b]
        tq = t0 + jnp.arange(Q_BLOCK)
        cur = t0 // P
        gate = jnp.einsum('qhd,hnd->qhn', qb.astype(jnp.float32), km)
        gate = jnp.where((jnp.arange(nb) < cur)[None, None, :], gate, NEG)
        _, sel = lax.top_k(gate, kk)
        k_sel = kb[hidx, sel]
        v_sel = vb[hidx, sel]
        k_own = lax.dynamic_index_in_dim(kb, cur, axis=1, keepdims=False)
        v_own = lax.dynamic_index_in_dim(vb, cur, axis=1, keepdims=False)
        scale = HEAD_DIM ** -0.5
        s_sel = jnp.einsum('qhd,qhrpd->qhrp', qb, k_sel).astype(jnp.float32) * scale
        s_own = jnp.einsum('qhd,hpd->qhp', qb, k_own).astype(jnp.float32) * scale
        pos_sel = sel[..., None] * P + blk_off
        pos_own = cur * P + blk_off
        s_sel = s_sel - slopes[None, :, None, None] * (tq[:, None, None, None] - pos_sel).astype(jnp.float32)
        s_own = s_own - slopes[None, :, None] * (tq[:, None, None] - pos_own[None, None, :]).astype(jnp.float32)
        s_sel = jnp.where((sel < cur)[..., None], s_sel, NEG)
        s_own = jnp.where((pos_own[None, :] <= tq[:, None])[:, None, :], s_own, NEG)
        logits = jnp.concatenate([s_sel.reshape(Q_BLOCK, H, kk * P), s_own], axis=-1)
        p = jax.nn.softmax(logits, axis=-1).astype(v.dtype)
        p_sel = p[..., :kk * P].reshape(Q_BLOCK, H, kk, P)
        p_own = p[..., kk * P:]
        return (jnp.einsum('qhrp,qhrpd->qhd', p_sel, v_sel)
                + jnp.einsum('qhp,hpd->qhd', p_own, v_own))

    out = lax.map(block, (q_chunks, b_ids, t0s))
    return out.reshape(B, S, H, D)

def dsa_stick_mixer(x, w_in, kv_norm, w_uk, w_uv, w_out):
    B, S, _ = x.shape
    widths = (A_HEADS * HEAD_DIM, A_KV_RANK, IDX_HEADS * IDX_DIM, IDX_DIM, IDX_HEADS,
              B_HEADS * HEAD_DIM, B_HEADS * HEAD_DIM, B_HEADS * HEAD_DIM)
    cuts = np.cumsum(widths)[:-1].tolist()
    q_a, c_kv, q_idx, k_idx, w_idx, q_b, k_b, v_b = jnp.split(x @ w_in, cuts, axis=-1)
    o_a = dsa_attention(q_a.reshape(B, S, A_HEADS, HEAD_DIM), rms_norm(c_kv, kv_norm),
                        q_idx.reshape(B, S, IDX_HEADS, IDX_DIM), k_idx,
                        w_idx * IDX_HEADS ** -0.5, w_uk, w_uv)
    o_b = stick_breaking_attention(q_b.reshape(B, S, B_HEADS, HEAD_DIM),
                                   k_b.reshape(B, S, B_HEADS, HEAD_DIM),
                                   v_b.reshape(B, S, B_HEADS, HEAD_DIM))
    o = jnp.concatenate([o_a.reshape(B, S, -1), o_b.reshape(B, S, -1)], axis=-1)
    return o @ w_out

def moba_mixer(x, w_in, w_out):
    B, S, _ = x.shape
    q, k, v = jnp.split(x @ w_in, 3, axis=-1)
    shp = (B, S, C_HEADS, HEAD_DIM)
    o = moba_attention(q.reshape(shp), k.reshape(shp), v.reshape(shp))
    return o.reshape(B, S, -1) @ w_out

def swiglu(x, w_gate, w_up, w_down):
    return (jax.nn.silu(x @ w_gate) * (x @ w_up)) @ w_down

def setup_inputs(seed: int = 0) -> dict:
    key = jax.random.key(seed)
    ks = jax.random.split(key, 16)
    n_even = (DEPTH + 1) // 2
    n_odd = DEPTH // 2
    f32 = jnp.float32
    nrm = lambda k, shp, s: jax.random.normal(k, shp, f32) * s
    return {
        "x": jax.random.normal(ks[0], (BATCH, SEQ, D_MODEL), f32),
        "even_w_in": nrm(ks[1], (n_even, D_MODEL, EVEN_IN), D_MODEL ** -0.5),
        "even_kv_norm": 1.0 + nrm(ks[2], (n_even, A_KV_RANK), 0.05),
        "even_w_uk": nrm(ks[3], (n_even, A_HEADS, HEAD_DIM, A_KV_RANK), A_KV_RANK ** -0.5),
        "even_w_uv": nrm(ks[4], (n_even, A_HEADS, A_KV_RANK, HEAD_DIM), A_KV_RANK ** -0.5),
        "even_w_out": nrm(ks[5], (n_even, D_MODEL, D_MODEL), D_MODEL ** -0.5 * DEEPNORM_BETA),
        "odd_w_in": nrm(ks[6], (n_odd, D_MODEL, ODD_IN), D_MODEL ** -0.5),
        "odd_w_out": nrm(ks[7], (n_odd, D_MODEL, D_MODEL), D_MODEL ** -0.5 * DEEPNORM_BETA),
        "ln_mix_g": 1.0 + nrm(ks[8], (DEPTH, D_MODEL), 0.05),
        "ln_mix_b": nrm(ks[9], (DEPTH, D_MODEL), 0.02),
        "ffn_gate": nrm(ks[10], (DEPTH, D_MODEL, D_FF), D_MODEL ** -0.5),
        "ffn_up": nrm(ks[11], (DEPTH, D_MODEL, D_FF), D_MODEL ** -0.5),
        "ffn_down": nrm(ks[12], (DEPTH, D_FF, D_MODEL), D_FF ** -0.5 * DEEPNORM_BETA),
        "ln_ffn_g": 1.0 + nrm(ks[13], (DEPTH, D_MODEL), 0.05),
        "ln_ffn_b": nrm(ks[14], (DEPTH, D_MODEL), 0.02),
    }

def reference(x, even_w_in, even_kv_norm, even_w_uk, even_w_uv, even_w_out, odd_w_in, odd_w_out,
              ln_mix_g, ln_mix_b, ffn_gate, ffn_up, ffn_down, ln_ffn_g, ln_ffn_b):
    h = x
    for i in range(DEPTH):
        j = i // 2
        if i % 2 == 0:
            m = dsa_stick_mixer(h, even_w_in[j], even_kv_norm[j], even_w_uk[j], even_w_uv[j], even_w_out[j])
        else:
            m = moba_mixer(h, odd_w_in[j], odd_w_out[j])
        h = layer_norm(DEEPNORM_ALPHA * h + m, ln_mix_g[i], ln_mix_b[i])
        f = swiglu(h, ffn_gate[i], ffn_up[i], ffn_down[i])
        h = layer_norm(DEEPNORM_ALPHA * h + f, ln_ffn_g[i], ln_ffn_b[i])
    return h


_drawn_inputs = setup_inputs


def setup_inputs(seed=0):
    import zlib

    import numpy as np

    out = dict(_drawn_inputs(seed))
    spreads = {}
    factors = {'even_kv_norm': 8.0}
    for name, (base, spread) in spreads.items():
        noise = np.random.default_rng([zlib.crc32(name.encode()), seed]).standard_normal(out[name].shape)
        drawn = base * np.exp(spread * noise) if base else spread * noise
        out[name] = __import__('jax').numpy.asarray(drawn.astype(out[name].dtype))
    for name, factor in factors.items():
        out[name] = (out[name] * factor).astype(out[name].dtype)
    return out
```

```python
from contextlib import ExitStack

import concourse.bass as bass
from concourse import mybir

F32 = mybir.dt.float32
F32R = mybir.dt.float32r
ALU = mybir.AluOpType
ACT = mybir.ActivationFunctionType
AX_X = mybir.AxisListType.X

P = 128
D = 1024
S = 256
KT = D // P
DH = 64
A_HEADS, B_HEADS, C_HEADS, I_HEADS = 8, 8, 16, 4
GH = 4
TOPK = min(256, S // 4)
DFF = -(-8 * D // (3 * 256)) * 256
FT = DFF // P
PAIRS = FT // 2
ALPHA = (2 * 2) ** 0.25
LN_EPS, RMS_EPS = 1e-5, 1e-6
CW = 2048
RING, RAW = 6, 2
AHEAD = 4
L0_IN, L0_OUT, L0_FFN = 0, 10, 14
L1_IN = L0_FFN + 3 * PAIRS
L1_OUT = L1_IN + 12
L1_FFN = L1_OUT + 4
CHUNKS = L1_FFN + 3 * PAIRS
NORM_CHUNK = (L0_OUT + 3, L1_IN - 1, L1_OUT + 3, CHUNKS - 1)
NEG = -1e30
MASKED = -1e38
TAKEN = -3e38
TRI = 3 * P


def build(nc, x, xT, stream, w_idx, w_uk, w_uv, kv_norm, ln_rows, ln_cols, consts, out):
    with ExitStack() as ctx:
        def sb(name, shape, dt=F32):
            return ctx.enter_context(nc.sbuf_tensor(name, shape, dt))

        def sem(name):
            return ctx.enter_context(nc.semaphore(name))

        raw = sb("raw", [P, RAW, CW])
        whi = sb("whi", [P, RING, CW], F32R)
        wlo = sb("wlo", [P, RING, CW], F32R)
        h = sb("h", [P, 2, D])
        hThi = sb("hThi", [P, KT, S], F32R)
        hTlo = sb("hTlo", [P, KT, S], F32R)
        oThi = sb("oThi", [P, KT, S], F32R)
        oTlo = sb("oTlo", [P, KT, S], F32R)
        ahi, alo = oThi, oTlo
        qT = sb("qT", [P, KT, S])
        kT = sb("kT", [P, KT, S])
        v = sb("v", [P, 2, D])
        hT = v[:].rearrange("p t (k s) -> p (t k) s", s=S)
        grow = qT[:, 0:4, :].rearrange("p k s -> p (k s)")
        brow = qT[:, 4:8, :].rearrange("p k s -> p (k s)")
        otok = sb("otok", [P, 2, 2 * S])
        prob = sb("prob", [P, 3, TRI])
        probT = sb("probT", [P, 2, TRI])
        scratch = sb("scratch", [P, 5, TRI])
        dist = sb("dist", [P, TRI + 3 * P])
        dsel = sb("dsel", [P, TRI])
        small = sb("small", [P, 192])
        wix = sb("wix", [P, KT, I_HEADS])
        ukv = sb("ukv", [P, 2, 4, P])
        kvrow = sb("kvrow", [P, P])
        zeros = sb("zeros", [P, P], F32R)
        bank = [ctx.enter_context(nc.psum_tensor(f"bank{b}", [P, 512], F32)) for b in range(8)]

        negtri = dist[:, TRI:TRI + P]
        negones = dist[:, TRI + P:TRI + 2 * P]
        ident = dist[:, TRI + 2 * P:TRI + 3 * P]
        dcaus = dist[:, 0:TRI]
        kiT, cT = kT[:, 4, :], kT[:, 5, :]
        craw, cn = v[:, :, 640:768], v[:, :, 512:640]
        sgate = scratch[:, 0:2, 0:S]
        aful = scratch[:, 2:4, 0:S]
        idx = scratch[:, 4, :]
        qlT = scratch[:, 0, 0:S]
        olT = scratch[:, 1, 0:S]
        lncol = small[:, 0:64].rearrange("p (n a k) -> p n a k", n=4, a=2)
        wq_i = small[:, 64:72].rearrange("p (t i) -> p t i", t=2)
        m8 = small[:, 72:88].rearrange("p (t e) -> p t e", t=2)
        nmax = small[:, 88:94].rearrange("p (b t) -> p b t", b=3)
        rsum = small[:, 96:112].rearrange("p (b t j) -> p b t j", b=2, t=2)
        rinv = small[:, 112:128].rearrange("p (b t j) -> p b t j", b=2, t=2)
        stats = small[:, 128:152].rearrange("p (t c) -> p t c", t=2)
        mv = small[:, 152:156].rearrange("p (t c) -> p t c", t=2)
        std = small[:, 156:158]
        rstd = small[:, 158:160]
        msq = small[:, 160:162]
        eps = small[:, 162:164]

        raw_loaded = [sem(f"raw_loaded{i}") for i in range(RAW)]
        x_loaded, xT_loaded, par_loaded, rows_loaded = (
            sem("x_loaded"), sem("xT_loaded"), sem("par_loaded"), sem("rows_loaded"))
        whi_ready, wlo_ready, chunk_used = sem("whi_ready"), sem("wlo_ready"), sem("chunk_used")
        hThi_ready, hTlo_ready, hT_ready = sem("hThi_ready"), sem("hTlo_ready"), sem("hT_ready")
        proj_evac = sem("proj_evac")
        eps_set = sem("eps_set")
        widx_done, widx_ready = sem("widx_done"), sem("widx_ready")
        msq_ready, cstd_ready, crstd_ready, c_ready, ctr_done, cT_ready = (
            sem("msq_ready"), sem("cstd_ready"), sem("crstd_ready"), sem("c_ready"), sem("ctr_done"), sem("cT_ready"))
        dots_done, relu_done, idx_step, idx_masked, topk_step, dsel_ready = (
            sem("dots_done"), sem("relu_done"), sem("idx_step"), sem("idx_masked"), sem("topk_step"),
            sem("dsel_ready"))
        qlat_done, qlat_ready = sem("qlat_done"), sem("qlat_ready")
        scores_done, logits_done, max_done, probs_ready = (
            sem("scores_done"), sem("logits_done"), sem("max_done"), sem("probs_ready"))
        probT_done, probT_ready, pv_done = sem("probT_done"), sem("probT_ready"), sem("pv_done")
        olat_done, olat_ready = sem("olat_done"), sem("olat_ready")
        rinv_ready, otok_ready, otr_done, oThi_ready, oTlo_ready = (
            sem("rinv_ready"), sem("otok_ready"), sem("otr_done"), sem("oThi_ready"), sem("oTlo_ready"))
        z_done, absz_ready, e_ready, l_ready, sp_ready, sp_masked, rem_done, a_exp, a_masked = (
            sem("z_done"), sem("absz_ready"), sem("e_ready"), sem("l_ready"), sem("sp_ready"), sem("sp_masked"),
            sem("rem_done"), sem("a_exp"), sem("a_masked"))
        acc0_done, res_done, stat_done, mv_ready, std_ready, rstd_ready, norm_ready = (
            sem("acc0_done"), sem("res_done"), sem("stat_done"), sem("mv_ready"), sem("std_ready"),
            sem("rstd_ready"), sem("norm_ready"))
        tr0_done, tr1_done, scaled, hres_ready = sem("tr0_done"), sem("tr1_done"), sem("scaled"), sem("hres_ready")
        gate_done, silu_ready, amul_ready, ahi_ready, alo_ready = (
            sem("gate_done"), sem("silu_ready"), sem("amul_ready"), sem("ahi_ready"), sem("alo_ready"))
        out_ready, stored = sem("out_ready"), sem("stored")

        block = ctx.enter_context(nc.Block())

        def start_unit(hd):
            return 6 * (hd // GH) + (0, 1, 3, 4)[hd % GH]

        C_AT = {start_unit(hd): hd for hd in range(C_HEADS)}
        C_UNITS = 2 * 12
        B_UNITS = B_HEADS + 3

        @block.sync
        def _(sp):
            for s in range(RAW):
                sp.dma_start(raw[:, s], stream[s]).then_inc(raw_loaded[s], 16)
            with sp.Fori(1, CHUNKS // RAW) as i:
                for s in range(RAW):
                    sp.wait_ge(wlo_ready, RAW * i + (s + 1 - RAW))
                    sp.dma_start(raw[:, s], stream[RAW * i + s]).then_inc(raw_loaded[s], 16)
            for t in range(2):
                sp.wait_ge(out_ready, t + 1)
                sp.dma_start(out[t], h[:, t]).then_inc(stored, 16)
            sp.wait_ge(stored, 32)

        @block.gpsimd
        def _(pool):
            pool.dma_start(dist[:], consts).then_inc(par_loaded, 16)
            pool.dma_start(wix[:], w_idx).then_inc(par_loaded, 16)
            pool.dma_start(kvrow[:], kv_norm.partition_broadcast(P)).then_inc(par_loaded, 16)
            pool.dma_start(lncol, ln_cols).then_inc(par_loaded, 16)
            pool.dma_start(ukv[:, 0], w_uk).then_inc(par_loaded, 16)
            pool.dma_start(ukv[:, 1], w_uv).then_inc(par_loaded, 16)
            pool.dma_start(h[:], x).then_inc(x_loaded, 16)
            nc.gpsimd.memset(zeros[:].bitcast(F32), 0.0)
            nc.gpsimd.memset(eps[:, 0:1], LN_EPS)
            nc.gpsimd.memset(eps[:, 1:2], RMS_EPS).then_inc(eps_set, 1)

            diag = idx.rearrange("p (b c) -> p b c", b=3)[:, 0:3:2, :]
            pool.wait_ge(idx_step, 2 * I_HEADS)
            nc.gpsimd.affine_select(out=diag, in_=diag, pattern=[[0, 2], [-1, P]], compare_op=ALU.is_ge, fill=NEG,
                                    base=0, channel_multiplier=1).then_inc(idx_masked, 1)

            def zero_future(t, done, n, ready):
                blocks = t.rearrange("p (b c) -> p b c", b=3)[:, 0:3:2, :]
                pool.wait_ge(done, n)
                nc.gpsimd.affine_select(out=blocks, in_=blocks, pattern=[[0, 2], [1, P]], compare_op=ALU.is_gt,
                                        fill=0.0, base=0, channel_multiplier=-1).then_inc(ready, 1)

            for m in range(B_UNITS):
                if m < B_HEADS:
                    zero_future(scratch[:, 2 + m % 3, :], sp_ready, m + 1, sp_masked)
                if 0 <= m - 2 < B_HEADS:
                    zero_future(prob[:, (m - 2) % 3, :], a_exp, m - 1, a_masked)

            for n in range(4):
                if n % 2 == 0:
                    pool.wait_ge(acc0_done, n + 1)
                else:
                    pool.wait_ge(hres_ready, 2 * n)
                pool.dma_start(grow, ln_rows[n, 0].partition_broadcast(P)).then_inc(rows_loaded, 16)
                pool.dma_start(brow, ln_rows[n, 1].partition_broadcast(P)).then_inc(rows_loaded, 16)
                pool.wait_ge(rows_loaded, 32 * (n + 1))
                for t in range(2 if n < 3 else 1):
                    if n == 3:
                        pool.wait_ge(norm_ready, 7)
                    elif t == 0:
                        pool.wait_ge(tr0_done, n + 1)
                    else:
                        pool.wait_ge(tr1_done, 4 * n + 4)
                    nc.gpsimd.tensor_tensor(h[:, t], h[:, t], grow, ALU.mult).then_inc(scaled, 1)
                    pool.wait_ge(scaled, 2 * n + t + 1)
                    nc.gpsimd.tensor_tensor(h[:, t], h[:, t], brow, ALU.add).then_inc(
                        hres_ready if n < 3 else out_ready, 1)

        @block.scalar
        def _(act):
            def split_hi(c, i=0):
                act.wait_ge(raw_loaded[c % RAW], 16 * (c // RAW + 1) + 16 * (RING // RAW) * i)
                if c >= RING or not isinstance(i, int):
                    act.wait_ge(chunk_used, c - RING + 1 + RING * i)
                nc.scalar.copy(whi[:, c % RING], raw[:, c % RAW]).then_inc(whi_ready, 1)

            def evac_proj(c, n, dst, scale=1.0):
                act.wait_ge(chunk_used, c + 1)
                nc.scalar.activation(dst, bank[4 + n % 2][:].rearrange("p (t c) -> p t c", t=2), ACT.Copy,
                                     scale=scale).then_inc(proj_evac, 1)

            def exp_rows(n, hd):
                act.wait_ge(max_done, 2 * n + 2)
                p = prob[:, n % 3]
                g = hd // GH
                if hd % GH == 0 and n >= 2 * GH:
                    act.wait_ge(rinv_ready, n // GH - 1)
                nc.scalar.activation(p[:, 0:P], p[:, 0:P], ACT.Exp, bias=nmax[:, n % 3, 0:1],
                                     accum_out=rsum[:, g % 2, 0, hd % GH:hd % GH + 1])
                nc.scalar.activation(p[:, P:TRI], p[:, P:TRI], ACT.Exp, bias=nmax[:, n % 3, 1:2],
                                     accum_out=rsum[:, g % 2, 1, hd % GH:hd % GH + 1]).then_inc(probs_ready, 1)

            def evac_probT(n):
                act.wait_ge(probT_done, n + 1)
                if n >= 2:
                    act.wait_ge(pv_done, n - 1)
                nc.scalar.copy(probT[:, n % 2], bank[1][:, 0:TRI]).then_inc(probT_ready, 1)

            def evac_oT_hi(G, kt):
                act.wait_ge(otr_done, G + 1)
                nc.scalar.copy(oThi[:, kt:kt + 2, :], bank[2 + G % 2][:].rearrange("p (k s) -> p k s", k=2)
                               ).then_inc(oThi_ready, 1)

            def split_hT(n):
                for b in range(4):
                    if n == 0:
                        if b == 0:
                            act.wait_ge(xT_loaded, 16)
                    else:
                        act.wait_ge(hT_ready, 8 * (n - 1) + 2 * b + 2)
                    nc.scalar.copy(hThi[:, 2 * b:2 * b + 2], hT[:, 2 * b:2 * b + 2]).then_inc(hThi_ready, 1)

            def norm_std(n):
                for t in range(2):
                    act.wait_ge(mv_ready, 2 * n + t + 1)
                    nc.scalar.activation(std[:, t:t + 1], mv[:, t, 1:2], ACT.Sqrt, bias=eps[:, 0:1]
                                         ).then_inc(std_ready, 1)

            act.dma_start(hT, xT).then_inc(xT_loaded, 16)
            split_hT(0)
            for c in range(AHEAD):
                split_hi(c)
            act.wait_ge(widx_done, 1)
            nc.scalar.activation(wq_i, bank[6][:, 0:8].rearrange("p (t i) -> p t i", t=2), ACT.Copy,
                                 scale=I_HEADS ** -0.5).then_inc(widx_ready, 1)
            act.wait_ge(chunk_used, 1)
            nc.scalar.copy(craw, bank[4][:, S:2 * S].rearrange("p (t c) -> p t c", t=2))
            nc.scalar.copy(kiT, bank[4][:, 0:S]).then_inc(proj_evac, 1)
            split_hi(4)
            evac_proj(1, 1, kT[:, 6:8, :])
            split_hi(5)
            act.wait_ge(eps_set, 1)
            act.wait_ge(msq_ready, 2)
            nc.scalar.activation(std[:, 0:2], msq, ACT.Sqrt, bias=eps[:, 1:2], scale=1.0 / P).then_inc(cstd_ready, 1)
            evac_proj(2, 2, qT[:, 4:6, :], DH ** -0.5)
            for i in range(I_HEADS):
                act.wait_ge(dots_done, i + 1)
                nc.scalar.activation(scratch[:, i, :], bank[i][:, 0:TRI], ACT.Relu, scale=DH ** -0.5
                                     ).then_inc(relu_done, 1)
            split_hi(6)
            evac_proj(3, 3, qT[:, 6:8, :], DH ** -0.5)
            split_hi(7)
            act.wait_ge(ctr_done, 1)
            nc.scalar.copy(cT, bank[6][:, 0:S]).then_inc(cT_ready, 1)

            for u in range(12):
                if 0 <= u - 3 < A_HEADS:
                    act.wait_ge(olat_done, u - 2)
                    if u - 3 >= 1:
                        act.wait_ge(pv_done, u - 3)
                    nc.scalar.copy(olT, bank[7][:, 0:S]).then_inc(olat_ready, 1)
                if 0 <= u - 2 < A_HEADS:
                    evac_probT(u - 2)
                if u < A_HEADS:
                    act.wait_ge(qlat_done, u + 1)
                    if u >= 1:
                        act.wait_ge(scores_done, u)
                    if u == 0:
                        act.wait_ge(idx_step, 2 * I_HEADS)
                    nc.scalar.copy(qlT, bank[6][:, 0:S]).then_inc(qlat_ready, 1)
                if 0 <= u - 1 < A_HEADS:
                    exp_rows(u - 1, u - 1)
                c = 4 + u // 2
                if u % 2 == 0:
                    split_hi(c + AHEAD)
                else:
                    g, what = (c - 4) // 3, (c - 4) % 3
                    if what == 0:
                        evac_proj(c, c, qT[:, 2 * g:2 * g + 2, :], DH ** -0.5)
                    elif what == 1:
                        evac_proj(c, c, kT[:, 2 * g:2 * g + 2, :])
                    else:
                        evac_proj(c, c, v[:, :, g * S:(g + 1) * S])
                if u == 8:
                    evac_oT_hi(0, 0)

            for m in range(B_UNITS):
                if m < B_HEADS:
                    e = scratch[:, m % 2, :]
                    act.wait_ge(z_done, m + 1)
                    if m >= 2:
                        act.wait_ge(sp_ready, m - 1)
                    nc.scalar.activation(e, bank[m % 2][:, 0:TRI], ACT.Abs).then_inc(absz_ready, 1)
                    act.wait_ge(absz_ready, m + 1)
                    nc.scalar.activation(e, e, ACT.Exp, scale=-1.0).then_inc(e_ready, 1)
                    act.wait_ge(e_ready, m + 1)
                    nc.scalar.activation(e, e, ACT.Ln, bias=1.0).then_inc(l_ready, 1)
                if m == 1:
                    evac_oT_hi(1, 2)
                if 0 <= m - 2 < B_HEADS:
                    act.wait_ge(rem_done, m - 1)
                    if m - 2 >= 3:
                        act.wait_ge(pv_done, A_HEADS + m - 4)
                    nc.scalar.activation(prob[:, (m - 2) % 3, :], bank[6 + m % 2][:, 0:TRI], ACT.Exp
                                         ).then_inc(a_exp, 1)
                if m == 8:
                    evac_oT_hi(2, 4)
            split_hi(L0_OUT + 4)
            split_hi(L0_OUT + 5)
            evac_oT_hi(3, 6)
            split_hi(L0_OUT + 6)
            split_hi(L0_OUT + 7)

            def ffn_tile(L, c, t, i=0, more=1):
                n = FT * L + t + 4 * i
                act.wait_ge(gate_done, n + 1)
                if t >= 2 or L:
                    act.wait_ge(amul_ready, n - 1)
                nc.scalar.activation(sgate[:, t % 2], bank[2 * (t % 2)][:, 0:S], ACT.Silu).then_inc(silu_ready, 1)
                if more:
                    split_hi(c + AHEAD, i)
                act.wait_ge(amul_ready, n + 1)
                nc.scalar.copy(ahi[:, t % 4, :], aful[:, t % 2]).then_inc(ahi_ready, 1)

            def ffn_body(L, i, upto=CHUNKS):
                base = L0_FFN if L == 0 else L1_FFN
                for j in range(2):
                    c = base + 2 + 3 * j
                    at = 0 if not isinstance(i, int) else 6 * i
                    ffn_tile(L, c, 2 + 2 * j, i, c + at + AHEAD < upto)
                    ffn_tile(L, c + 1, 3 + 2 * j, i, c + at + 1 + AHEAD < upto)
                    if c + at + 2 + AHEAD < upto:
                        split_hi(c + 2 + AHEAD, i)

            def ffn(L):
                base = L0_FFN if L == 0 else L1_FFN
                for t in range(2):
                    ffn_tile(L, base + t, t)
                loops = (PAIRS - 1) // 2 - L
                with act.Fori(0, loops) as i:
                    ffn_body(L, i)
                if L:
                    ffn_body(L, loops)
                else:
                    split_hi(base + 3 * PAIRS - 1 + AHEAD)

            norm_std(0)
            split_hT(1)
            ffn(0)
            norm_std(1)
            split_hT(2)

            def evac_l1(q):
                g, what = q // 3, q % 3
                dst = (qT[:, 2 * g:2 * g + 2, :], kT[:, 2 * g:2 * g + 2, :], v[:, :, g * S:(g + 1) * S])[what]
                if q == 0:
                    act.wait_ge(hres_ready, 4)
                evac_proj(L1_IN + q, 10 + q, dst, DH ** -0.5 if what == 0 else 1.0)

            for q in range(3):
                split_hi(L1_IN + q + AHEAD)
                evac_l1(q)
            for u in range(C_UNITS + 1):
                if u - 1 in C_AT:
                    evac_probT(A_HEADS + C_AT[u - 1])
                if u in C_AT:
                    exp_rows(A_HEADS + C_AT[u], C_AT[u])
                if u % 2 == 0 and u < C_UNITS:
                    split_hi(L1_IN + 3 + u // 2 + AHEAD)
                if u % 2 == 1 and u < 18:
                    evac_l1(3 + u // 2)
                if u >= 8 and (u - 8) % 6 == 0:
                    evac_oT_hi(4 + (u - 8) // 6, 2 * ((u - 8) // 6))
            evac_oT_hi(7, 6)
            split_hi(L1_OUT + 3 + AHEAD)
            norm_std(2)
            split_hT(3)
            ffn(1)
            norm_std(3)

        @block.vector
        def _(dve):
            chained = [0]

            def split_lo(c, i=0):
                dve.wait_ge(whi_ready, c + 1 + RING * i)
                nc.vector.tensor_tensor(wlo[:, c % RING], raw[:, c % RAW], whi[:, c % RING].bitcast(F32),
                                        ALU.subtract).then_inc(wlo_ready, 1)

            def split_hT(n, b):
                dve.wait_ge(hThi_ready, 4 * n + b + 1)
                nc.vector.tensor_tensor(hTlo[:, 2 * b:2 * b + 2], hT[:, 2 * b:2 * b + 2],
                                        hThi[:, 2 * b:2 * b + 2].bitcast(F32), ALU.subtract).then_inc(hTlo_ready, 1)

            def logits(n, slope, table):
                dve.wait_ge(scores_done, n + 1)
                if n >= 3:
                    dve.wait_ge(probT_done, n - 2)
                p = prob[:, n % 3]
                nc.vector.scalar_tensor_tensor(out=p, in0=table, scalar=float(slope), in1=bank[0][:, 0:TRI],
                                               op0=ALU.mult, op1=ALU.add).then_inc(logits_done, 1)
                dve.wait_ge(logits_done, n + 1)
                nc.vector.tensor_reduce(nmax[:, n % 3, 0:1], p[:, 0:P], AX_X, ALU.max, negate=True
                                        ).then_inc(max_done, 1)
                nc.vector.tensor_reduce(nmax[:, n % 3, 1:2], p[:, P:TRI], AX_X, ALU.max, negate=True
                                        ).then_inc(max_done, 1)

            def normalise(G, ng, pvs):
                b = ng % 2
                dve.wait_ge(pv_done, pvs)
                nc.vector.reciprocal(rinv[:, b], rsum[:, b]).then_inc(rinv_ready, 1)
                dve.wait_ge(rinv_ready, ng + 1)
                nc.vector.tensor_tensor(
                    otok[:, G % 2].rearrange("p (a d) -> p a d", d=DH),
                    bank[2 + G % 2][:].rearrange("p (a d) -> p a d", d=DH),
                    rinv[:, b].rearrange("p t j -> p (t j)").unsqueeze(2).to_broadcast([P, 2 * GH, DH]),
                    ALU.mult).then_inc(otok_ready, 1)

            def evac_oT_lo(G, kt):
                dve.wait_ge(oThi_ready, G + 1)
                nc.vector.tensor_tensor(oTlo[:, kt:kt + 2, :], bank[2 + G % 2][:].rearrange("p (k s) -> p k s", k=2),
                                        oThi[:, kt:kt + 2, :].bitcast(F32), ALU.subtract).then_inc(oTlo_ready, 1)

            def norm(n, last=False):
                for t in range(2):
                    k = 2 * n + t
                    if t == 0:
                        dve.wait_ge(acc0_done, n + 1)
                    else:
                        dve.wait_ge(chunk_used, NORM_CHUNK[n] + 1)
                    if n == 0:
                        dve.wait_ge(x_loaded, 16)
                    else:
                        dve.wait_ge(hres_ready, 2 * n)
                    for a in range(2):
                        hh = h[:, t, a * 512:(a + 1) * 512]
                        nc.vector.scalar_tensor_tensor(out=hh, in0=hh, scalar=ALPHA, in1=bank[4 + 2 * t + a][:],
                                                       op0=ALU.mult, op1=ALU.add).then_inc(res_done, 1)
                    for a in range(2):
                        dve.wait_ge(res_done, 2 * k + a + 1)
                        nc.vector.bn_stats(stats[:, t, 6 * a:6 * a + 6], h[:, t, a * 512:(a + 1) * 512]
                                           ).then_inc(stat_done, 1)
                    dve.wait_ge(stat_done, 2 * k + 2)
                    nc.vector.bn_aggr(mv[:, t], stats[:, t]).then_inc(mv_ready, 1)
                    dve.wait_ge(std_ready, k + 1)
                    nc.vector.reciprocal(rstd[:, t:t + 1], std[:, t:t + 1]).then_inc(rstd_ready, 1)
                    dve.wait_ge(rstd_ready, k + 1)
                    nc.vector.tensor_scalar(h[:, t], h[:, t], mv[:, t, 0:1], rstd[:, t:t + 1], ALU.subtract,
                                            ALU.mult).then_inc(norm_ready, 1)
                if last:
                    return
                for k in range(KT):
                    dve.wait_ge(tr1_done, 4 * n + k // 2 + 1)
                    nc.vector.tensor_scalar(hT[:, k, :], bank[k // 2][:, (k % 2) * S:(k % 2 + 1) * S],
                                            lncol[:, n, 0, k:k + 1], lncol[:, n, 1, k:k + 1], ALU.mult,
                                            ALU.add).then_inc(hT_ready, 1)
                    if k % 2 == 1 and k >= 3:
                        split_hT(n + 1, k // 2 - 1)
                split_hT(n + 1, 3)

            for b in range(4):
                split_hT(0, b)
            for c in range(AHEAD + 1):
                split_lo(c)
            dve.wait_ge(proj_evac, 1)
            for t in range(2):
                nc.vector.scalar_tensor_tensor(out=cn[:, t], in0=craw[:, t], scalar=1.0, in1=craw[:, t],
                                               op0=ALU.mult, op1=ALU.mult, accum_out=msq[:, t:t + 1]
                                               ).then_inc(msq_ready, 1)
            split_lo(5)
            dve.wait_ge(cstd_ready, 1)
            nc.vector.reciprocal(rstd, std).then_inc(crstd_ready, 1)
            dve.wait_ge(crstd_ready, 1)
            dve.wait_ge(par_loaded, 96)
            for t in range(2):
                nc.vector.scalar_tensor_tensor(out=cn[:, t], in0=craw[:, t], scalar=rstd[:, t:t + 1], in1=kvrow[:],
                                               op0=ALU.mult, op1=ALU.mult).then_inc(c_ready, 1)
            cols = (slice(0, P), slice(P, TRI))
            dve.wait_ge(widx_ready, 1)
            for i in range(I_HEADS):
                dve.wait_ge(relu_done, i + 1)
                for t in range(2):
                    w = wq_i[:, t, i:i + 1]
                    if i == 0:
                        op = nc.vector.tensor_scalar(idx[:, cols[t]], scratch[:, i, cols[t]], w, None, ALU.mult)
                    else:
                        dve.wait_ge(idx_step, 2 * i - 1 + t)
                        op = nc.vector.scalar_tensor_tensor(out=idx[:, cols[t]], in0=scratch[:, i, cols[t]],
                                                            scalar=w, in1=idx[:, cols[t]], op0=ALU.mult,
                                                            op1=ALU.add)
                    op.then_inc(idx_step, 1)
            split_lo(6)
            dve.wait_ge(idx_masked, 1)
            done = 0
            for r in range(TOPK // 8):
                for t in range(2):
                    if r:
                        dve.wait_ge(topk_step, 4 * r - 1 + t)
                    nc.vector.max(m8[:, t], idx[:, cols[t]]).then_inc(topk_step, 1)
                for t in range(2):
                    dve.wait_ge(topk_step, 4 * r + 1 + t)
                    nc.vector.match_replace(idx[:, cols[t]], m8[:, t], idx[:, cols[t]], TAKEN
                                            ).then_inc(topk_step, 1)
                if r == 3:
                    split_lo(7)
            dve.wait_ge(topk_step, 4 * (TOPK // 8))
            nc.vector.tensor_scalar(dsel[:], idx, TAKEN / 1.5, MASKED, ALU.is_gt, ALU.mult).then_inc(dsel_ready, 1)
            dve.wait_ge(dsel_ready, 1)
            nc.vector.tensor_tensor(dsel[:], dsel[:], dcaus, ALU.add).then_inc(dsel_ready, 1)
            dve.wait_ge(dsel_ready, 2)

            for u in range(12):
                if 0 <= u - 1 < A_HEADS:
                    logits(u - 1, 2.0 ** (-8.0 * u / A_HEADS), dsel[:])
                if u % 2 == 0:
                    split_lo(4 + u // 2 + AHEAD)
                if u == 7:
                    normalise(0, 0, GH)
                if u == 8:
                    evac_oT_lo(0, 0)
                if u == 11:
                    normalise(1, 1, 2 * GH)

            for m in range(B_UNITS):
                if m < B_HEADS:
                    e = scratch[:, m % 2, :]
                    dve.wait_ge(l_ready, m + 1)
                    if m >= 3:
                        dve.wait_ge(rem_done, m - 2)
                    nc.vector.scalar_tensor_tensor(out=scratch[:, 2 + m % 3, :], in0=bank[m % 2][:, 0:TRI],
                                                   scalar=0.0, in1=e, op0=ALU.max, op1=ALU.add
                                                   ).then_inc(sp_ready, 1)
                if m == 1:
                    evac_oT_lo(1, 2)
                if m in (6, 10):
                    G = 2 + (m - 6) // 4
                    dve.wait_ge(pv_done, A_HEADS + m - 2)
                    nc.vector.tensor_copy(otok[:, G % 2], bank[2 + G % 2][:]).then_inc(otok_ready, 1)
                if m == 8:
                    evac_oT_lo(2, 4)
            split_lo(L0_OUT + 4)
            split_lo(L0_OUT + 5)
            evac_oT_lo(3, 6)
            split_lo(L0_OUT + 6)
            split_lo(L0_OUT + 7)

            def ffn_tile(L, c, t, i=0, more=1):
                n = FT * L + t + 4 * i
                dve.wait_ge(silu_ready, n + 1)
                dve.wait_ge(chunk_used, c + 1 + RING * i)
                if t >= 2 or L:
                    dve.wait_ge(alo_ready, n - 1)
                nc.vector.tensor_tensor(aful[:, t % 2], sgate[:, t % 2], bank[2 * (t % 2) + 1][:, 0:S], ALU.mult
                                        ).then_inc(amul_ready, 1)
                if more:
                    split_lo(c + AHEAD, i)
                dve.wait_ge(ahi_ready, n + 1)
                nc.vector.tensor_tensor(alo[:, t % 4, :], aful[:, t % 2], ahi[:, t % 4, :].bitcast(F32),
                                        ALU.subtract).then_inc(alo_ready, 1)

            def ffn_body(L, i, upto=CHUNKS):
                base = L0_FFN if L == 0 else L1_FFN
                for j in range(2):
                    c = base + 2 + 3 * j
                    at = 0 if not isinstance(i, int) else 6 * i
                    ffn_tile(L, c, 2 + 2 * j, i, c + at + AHEAD < upto)
                    ffn_tile(L, c + 1, 3 + 2 * j, i, c + at + 1 + AHEAD < upto)
                    if c + at + 2 + AHEAD < upto:
                        split_lo(c + 2 + AHEAD, i)

            def ffn(L):
                base = L0_FFN if L == 0 else L1_FFN
                for t in range(2):
                    ffn_tile(L, base + t, t)
                loops = (PAIRS - 1) // 2 - L
                with dve.Fori(0, loops) as i:
                    ffn_body(L, i)
                if L:
                    ffn_body(L, loops)
                else:
                    split_lo(base + 3 * PAIRS - 1 + AHEAD)

            norm(0)
            ffn(0)
            norm(1)

            for q in range(3):
                split_lo(L1_IN + q + AHEAD)
            for u in range(C_UNITS + 1):
                if u in C_AT:
                    hd = C_AT[u]
                    logits(A_HEADS + hd, 2.0 ** (-8.0 * (hd + 1) / C_HEADS), dcaus)
                if u % 2 == 0 and u < C_UNITS:
                    split_lo(L1_IN + 3 + u // 2 + AHEAD)
                if u >= 6 and u % 6 == 0:
                    g = u // 6 - 1
                    normalise(4 + g, 2 + g, A_HEADS + B_HEADS + GH * (g + 1))
                if u >= 8 and (u - 8) % 6 == 0:
                    g = (u - 8) // 6
                    evac_oT_lo(4 + g, 2 * g)
            evac_oT_lo(7, 6)
            split_lo(L1_OUT + 3 + AHEAD)
            norm(2)
            ffn(1)
            norm(3, last=True)
            dve.wait_ge(norm_ready, 8)
            dve.wait_ge(rows_loaded, 128)
            nc.vector.tensor_tensor(h[:, 1], h[:, 1], grow, ALU.mult).then_inc(norm_ready, 1)
            dve.wait_ge(norm_ready, 9)
            dve.wait_ge(out_ready, 1)
            nc.vector.tensor_tensor(h[:, 1], h[:, 1], brow, ALU.add).then_inc(out_ready, 1)

        @block.tensor
        def _(pe):
            mm = nc.tensor.matmul
            HT_PASSES = ((whi, hThi), (whi, hTlo), (wlo, hThi))
            AT_PASSES = ((whi, ahi), (whi, alo), (wlo, ahi))

            def chunk(c, i=0):
                pe.wait_ge(wlo_ready, c + 1 + RING * i)

            def cols_out(dst, slot, off, n=None):
                for k in range(KT):
                    if n is not None and k % 2 == 0:
                        pe.wait_ge(hTlo_ready, 4 * n + k // 2 + 1)
                    for j, (w, a) in enumerate(HT_PASSES):
                        last = mm(dst, w[:, slot, off + k * P:off + (k + 1) * P], a[:, k, :],
                                  start=(k == 0 and j == 0), stop=(k == KT - 1 and j == 2))
                return last

            def rows_out(dst, slot, off, t, width):
                for k in range(KT):
                    for j, (w, a) in enumerate(HT_PASSES):
                        last = mm(dst, a[:, k, t * P:(t + 1) * P], w[:, slot, off + k * width:off + (k + 1) * width],
                                  start=(k == 0 and j == 0), stop=(k == KT - 1 and j == 2))
                return last

            def proj_half(c, n, half, is_v, src=None):
                if half == 0:
                    chunk(c)
                    if n >= 2:
                        pe.wait_ge(proj_evac, n - 1)
                dst = bank[4 + n % 2][:, half * S:(half + 1) * S]
                if is_v:
                    last = rows_out(dst, c % RING, 0, half, S)
                else:
                    last = cols_out(dst, c % RING, half * KT * P, src if half == 0 else None)
                if half == 1:
                    last.then_inc(chunk_used, 1)

            def out_tile(c, j, kt, acc_in, start, stop, toks=(0, 1)):
                for t in toks:
                    for a in range(2):
                        for q, (w, o) in enumerate(acc_in):
                            last = mm(bank[4 + 2 * t + a][:], o[:, kt, t * P:(t + 1) * P],
                                      w[:, c % RING, j * D + a * 512:j * D + (a + 1) * 512],
                                      start=(start and q == 0), stop=(stop and q == 2), skip_group_check=True)
                return last

            def last_out(c, kts, n):
                for t in range(2):
                    for j in range(2):
                        last = out_tile(c, j, kts[j], AT_PASSES, False, j == 1, toks=(t,))
                    if t == 0:
                        last.then_inc(acc0_done, 1)
                last.then_inc(chunk_used, 1)

            def transpose_group(G):
                pe.wait_ge(otok_ready, G + 1)
                for k in range(2):
                    for t in range(2):
                        last = nc.tensor.transpose(bank[2 + G % 2][:, k * S + t * P:k * S + (t + 1) * P],
                                                   otok[:, G % 2, t * S + k * P:t * S + (k + 1) * P], ident)
                last.then_inc(otr_done, 1)

            def transpose_probs(n):
                pe.wait_ge(probs_ready, n + 1)
                if n >= 1:
                    pe.wait_ge(probT_ready, n)
                for b in range(3):
                    last = nc.tensor.transpose(bank[1][:, b * P:(b + 1) * P], prob[:, n % 3, b * P:(b + 1) * P],
                                               ident)
                last.then_inc(probT_done, 1)

            def free_group_bank(G):
                if G >= 2:
                    pe.wait_ge(oTlo_ready, G - 1)

            pe.wait_ge(xT_loaded, 16)
            pe.wait_ge(par_loaded, 96)
            for t in range(2):
                for k in range(KT):
                    last = mm(bank[6][:, t * I_HEADS:(t + 1) * I_HEADS], hT[:, k, t * P:(t + 1) * P], wix[:, k, :],
                              start=(k == 0), stop=(k == KT - 1))
            last.then_inc(widx_done, 1)
            chunk(0)
            cols_out(bank[4][:, 0:S], 0, 0, 0)
            for t in range(2):
                last = rows_out(bank[4][:, S + t * P:S + (t + 1) * P], 0, KT * P, t, P)
            last.then_inc(chunk_used, 1)
            for c in range(1, 3):
                for half in range(2):
                    proj_half(c, c, half, False)
            pe.wait_ge(proj_evac, 2)
            for i in range(I_HEADS):
                p = DH * (i % 2)
                for t in range(2):
                    last = mm(bank[i][:, t * P:t * P + (t + 1) * P], kT[p:p + DH, 6 + i // 2, t * P:(t + 1) * P],
                              kiT[p:p + DH, 0:(t + 1) * P], start=True, stop=True)
                last.then_inc(dots_done, 1)
            for half in range(2):
                proj_half(3, 3, half, False)
            pe.wait_ge(c_ready, 2)
            pe.wait_ge(widx_ready, 1)
            for t in range(2):
                last = nc.tensor.transpose(bank[6][:, t * P:(t + 1) * P], cn[:, t], ident)
            last.then_inc(ctr_done, 1)

            pe.wait_ge(relu_done, I_HEADS)
            for u in range(12):
                c = 4 + u // 2
                proj_half(c, c, u % 2, (c - 4) % 3 == 2)
                if 0 <= u - 4 < A_HEADS:
                    hd = u - 4
                    pe.wait_ge(olat_ready, hd + 1)
                    if hd % GH == 0:
                        free_group_bank(hd // GH)
                    for t in range(2):
                        at = t * S + (hd % GH) * DH
                        last = mm(bank[2 + hd // GH][:, at:at + DH], olT[:, t * P:(t + 1) * P],
                                  ukv[:, 1].rearrange("p a b -> p (a b)")[:, hd * DH:(hd + 1) * DH], start=True,
                                  stop=True)
                    last.then_inc(pv_done, 1)
                if 0 <= u - 3 < A_HEADS:
                    n = u - 3
                    pe.wait_ge(probT_ready, n + 1)
                    if n >= 1:
                        pe.wait_ge(olat_ready, n)
                    mm(bank[7][:, 0:P], cn[:, 0], probT[:, n % 2, 0:P], start=True, stop=True)
                    mm(bank[7][:, P:S], cn[:, 0], probT[:, n % 2, P:S], start=True, stop=False)
                    mm(bank[7][:, P:S], cn[:, 1], probT[:, n % 2, S:TRI], start=False, stop=True
                       ).then_inc(olat_done, 1)
                if 0 <= u - 2 < A_HEADS:
                    transpose_probs(u - 2)
                if 0 <= u - 1 < A_HEADS:
                    n = u - 1
                    pe.wait_ge(qlat_ready, n + 1)
                    pe.wait_ge(cT_ready, 1)
                    if n >= 1:
                        pe.wait_ge(logits_done, n)
                    for t in range(2):
                        last = mm(bank[0][:, t * P:t * P + (t + 1) * P], qlT[:, t * P:(t + 1) * P],
                                  cT[:, 0:(t + 1) * P], start=True, stop=True)
                    last.then_inc(scores_done, 1)
                if u < A_HEADS:
                    p = DH * (u % 2)
                    if u == 0:
                        pe.wait_ge(proj_evac, 4)
                        pe.wait_ge(cT_ready, 1)
                    else:
                        pe.wait_ge(qlat_ready, u)
                    mm(bank[6][:, 0:S], ukv[p:p + DH, 0].rearrange("p a b -> p (a b)")[:, (u // 2) * P:(u // 2 + 1) * P],
                       qT[p:p + DH, 4 + u // 2, :], start=True, stop=True).then_inc(qlat_done, 1)
                if u == 8:
                    transpose_group(0)

            def z_product(b, p, jt, start, stop):
                mm(bank[b][:, 0:S], kT[p:p + DH, jt, 0:P], qT[p:p + DH, jt, :], start=start, stop=stop,
                   skip_group_check=True)
                return mm(bank[b][:, S:TRI], kT[p:p + DH, jt, P:S], qT[p:p + DH, jt, P:S], start=start, stop=stop,
                          skip_group_check=True)

            for m in range(B_UNITS):
                if m < B_HEADS:
                    pe.wait_ge(proj_evac, 6 + 3 * (m // GH))
                    if m >= 2:
                        pe.wait_ge(sp_ready, m - 1)
                    z_product(m % 2, DH * (m % 2), m // 2, True, True).then_inc(z_done, 1)
                if m == 1:
                    transpose_group(1)
                if 0 <= m - 2 < B_HEADS:
                    n = m - 2
                    sp_t = scratch[:, 2 + n % 3, :]
                    r = bank[6 + n % 2]
                    pe.wait_ge(sp_masked, n + 1)
                    if n >= 2:
                        pe.wait_ge(a_exp, n - 1)
                    mm(r[:, 0:S], negtri, sp_t[:, 0:S], start=True, stop=False, skip_group_check=True)
                    mm(r[:, P:S], negones, sp_t[:, S:TRI], start=False, stop=False, skip_group_check=True)
                    mm(r[:, S:TRI], negtri, sp_t[:, S:TRI], start=False, stop=False, skip_group_check=True)
                    z_product(6 + n % 2, DH * (n % 2), n // 2, False, True).then_inc(rem_done, 1)
                if 0 <= m - 3 < B_HEADS:
                    n = m - 3
                    G = 2 + n // GH
                    if n % GH == 0:
                        free_group_bank(G)
                        pe.wait_ge(proj_evac, 7 + 3 * (n // GH))
                    pe.wait_ge(a_masked, n + 1)
                    a = prob[:, n % 3, :]
                    vh = slice(n * DH, (n + 1) * DH)
                    o = bank[2 + G % 2]
                    at = (n % GH) * DH
                    mm(o[:, at:at + DH], a[:, 0:P], v[:, 0, vh], start=True, stop=True)
                    mm(o[:, S + at:S + at + DH], a[:, P:S], v[:, 0, vh], start=True, stop=False)
                    mm(o[:, S + at:S + at + DH], a[:, S:TRI], v[:, 1, vh], start=False, stop=True
                       ).then_inc(pv_done, 1)
                if m == 8:
                    transpose_group(2)

            for q in range(3):
                c = L0_OUT + q
                chunk(c)
                pe.wait_ge(oTlo_ready, q + 1)
                for j in range(2):
                    last = out_tile(c, j, 2 * q + j, AT_PASSES, q == 0 and j == 0, False)
                last.then_inc(chunk_used, 1)
                if q == 1:
                    transpose_group(3)
            chunk(L0_OUT + 3)
            pe.wait_ge(oTlo_ready, 4)
            last_out(L0_OUT + 3, (6, 7), 0)

            def norm_transposes(n):
                for t in range(2):
                    pe.wait_ge(norm_ready, 2 * n + t + 1)
                    for k in range(KT):
                        last = nc.tensor.transpose(bank[k // 2][:, (k % 2) * S + t * P:(k % 2) * S + (t + 1) * P],
                                                   h[:, t, k * P:(k + 1) * P], ident)
                        if t == 1 and k % 2 == 1:
                            last.then_inc(tr1_done, 1)
                    if t == 0:
                        last.then_inc(tr0_done, 1)

            def gate_up(L, c, t, i=0, src=None):
                n = FT * L + t + 4 * i
                chunk(c, i)
                if t >= 2:
                    pe.wait_ge(amul_ready, n - 1)
                cols_out(bank[2 * (t % 2)][:, 0:S], c % RING, 0, src).then_inc(gate_done, 1)
                cols_out(bank[2 * (t % 2) + 1][:, 0:S], c % RING, KT * P).then_inc(chunk_used, 1)

            def down(L, c, p, i=0):
                chunk(c, i)
                pe.wait_ge(alo_ready, FT * L + 2 * p + 2 + 4 * i)
                for j in range(2):
                    last = out_tile(c, j, (2 * p + j) % 4, AT_PASSES, False, False)
                last.then_inc(chunk_used, 1)

            def ffn(L, n):
                base = L0_FFN if L == 0 else L1_FFN
                norm_transposes(n)
                for t in range(2):
                    if t == 0:
                        pe.wait_ge(hTlo_ready, 4 * (n + 1) + 4)
                        for b in range(4):
                            mm(bank[4 + b][:], zeros[:], hThi[:, 0:2, :], start=True, stop=False,
                               skip_group_check=True)
                    gate_up(L, base + t, t, 0, n + 1 if t == 0 else None)
                with pe.Fori(0, (PAIRS - 1) // 2) as i:
                    for j in range(2):
                        c = base + 2 + 3 * j
                        gate_up(L, c, 2 + 2 * j, i)
                        gate_up(L, c + 1, 3 + 2 * j, i)
                        down(L, c + 2, j, i)
                c = base + 3 * PAIRS - 1
                chunk(c)
                pe.wait_ge(alo_ready, FT * (L + 1))
                last_out(c, ((FT - 2) % 4, (FT - 1) % 4), n + 1)

            ffn(0, 0)

            norm_transposes(1)
            for q in range(3):
                for half in range(2):
                    if q == 0 and half == 0:
                        pe.wait_ge(hTlo_ready, 12)
                    proj_half(L1_IN + q, 10 + q, half, q == 2)
            for u in range(C_UNITS + 1):
                if u < 18:
                    q = 3 + u // 2
                    proj_half(L1_IN + q, 10 + q, u % 2, q % 3 == 2)
                elif u < C_UNITS:
                    q = (u - 18) // 2
                    j = u % 2
                    if j == 0:
                        chunk(L1_OUT + q)
                        pe.wait_ge(oTlo_ready, 4 + q + 1)
                    if u == 18:
                        pe.wait_ge(proj_evac, 22)
                    last = out_tile(L1_OUT + q, j, 2 * q + j, AT_PASSES, u == 18, False)
                    if j == 1:
                        last.then_inc(chunk_used, 1)
                if u - 2 in C_AT:
                    hd = C_AT[u - 2]
                    n = A_HEADS + hd
                    G = 4 + hd // GH
                    if hd % GH == 0:
                        free_group_bank(G)
                        pe.wait_ge(proj_evac, 10 + 3 * (hd // GH) + 3)
                    pe.wait_ge(probT_ready, n + 1)
                    pt = probT[:, n % 2]
                    vh = slice(hd * DH, (hd + 1) * DH)
                    o = bank[2 + G % 2]
                    at = (hd % GH) * DH
                    mm(o[:, at:at + DH], pt[:, 0:P], v[:, 0, vh], start=True, stop=True)
                    mm(o[:, S + at:S + at + DH], pt[:, P:S], v[:, 0, vh], start=True, stop=False)
                    mm(o[:, S + at:S + at + DH], pt[:, S:TRI], v[:, 1, vh], start=False, stop=True
                       ).then_inc(pv_done, 1)
                if u - 1 in C_AT:
                    transpose_probs(A_HEADS + C_AT[u - 1])
                if u in C_AT:
                    hd = C_AT[u]
                    n = A_HEADS + hd
                    pe.wait_ge(proj_evac, 10 + 3 * (hd // GH) + 2)
                    pe.wait_ge(logits_done, n)
                    p = DH * (hd % 2)
                    for t in range(2):
                        last = mm(bank[0][:, t * P:t * P + (t + 1) * P], qT[p:p + DH, hd // 2, t * P:(t + 1) * P],
                                  kT[p:p + DH, hd // 2, 0:(t + 1) * P], start=True, stop=True)
                    last.then_inc(scores_done, 1)
                if u >= 8 and (u - 8) % 6 == 0:
                    transpose_group(4 + (u - 8) // 6)
            transpose_group(7)
            chunk(L1_OUT + 3)
            pe.wait_ge(oTlo_ready, 8)
            last_out(L1_OUT + 3, (6, 7), 2)
            ffn(1, 2)


def _blocks(w, cols):
    return w[:, cols].reshape(KT, P, -1).transpose(1, 0, 2)


def _tiles(w, start, n):
    import numpy as np
    return np.stack([_blocks(w, slice(start + P * j, start + P * (j + 1))) for j in range(n)], 1)


def _rows(w, kt):
    return w[kt * P:(kt + 2) * P].reshape(2, P, -1).transpose(1, 0, 2)


def weight_stream(w_in0, w_out0, w_in1, w_out1, gate, up, down):
    import numpy as np
    ckv, qi, ki, qb = 512, 640, 896, 964
    kb, vb = qb + 512, qb + 1024
    chunks = []

    def add(*parts):
        chunks.append(np.concatenate([p.reshape(P, -1) for p in parts], 1))

    kdup = np.concatenate([w_in0[:, ki:ki + DH]] * 2, 1)
    add(_tiles(kdup, 0, 1), _blocks(w_in0, slice(ckv, ckv + P)))
    add(_tiles(w_in0, qi, 2))
    add(_tiles(w_in0, 0, 2))
    add(_tiles(w_in0, 256, 2))
    for g in range(2):
        add(_tiles(w_in0, qb + S * g, 2))
        add(_tiles(w_in0, kb + S * g, 2))
        add(_blocks(w_in0, slice(vb + S * g, vb + S * (g + 1))))

    def out_rows(w):
        for q in range(4):
            add(_rows(w, 2 * q))

    def ffn(L):
        def gu(t):
            add(_tiles(gate[L], t * P, 1), _tiles(up[L], t * P, 1))
        gu(0)
        gu(1)
        for p in range(1, PAIRS):
            gu(2 * p)
            gu(2 * p + 1)
            add(_rows(down[L], 2 * (p - 1)))
        add(_rows(down[L], 2 * (PAIRS - 1)))

    out_rows(w_out0)
    ffn(0)
    for g in range(4):
        add(_tiles(w_in1, S * g, 2))
        add(_tiles(w_in1, D + S * g, 2))
        add(_blocks(w_in1, slice(2 * D + S * g, 2 * D + S * (g + 1))))
    out_rows(w_out1)
    ffn(1)
    return np.stack(chunks)


def constants():
    import numpy as np
    q = np.arange(P)[:, None]
    k = np.arange(P)[None, :]
    near = np.where(k <= q, k - q, MASKED)
    far = k - (q + P)
    tri = np.where(q >= k, -1.0, 0.0)
    return np.concatenate([near, far, near, tri, -np.ones((P, P)), np.eye(P)], 1).astype(np.float32)


def kernel(**inputs):
    import numpy as np
    import concourse.bacc as bacc
    from concourse.bass_utils import run_bass_kernel_spmd

    a = {k: np.asarray(w) for k, w in inputs.items()}
    xx = a["x"][0]
    w0 = a["even_w_in"][0]
    arrays = {
        "x_in": xx.reshape(2, P, D).transpose(1, 0, 2),
        "xT_in": xx.T.reshape(KT, P, S).transpose(1, 0, 2),
        "stream_in": weight_stream(w0, a["even_w_out"][0], a["odd_w_in"][0], a["odd_w_out"][0], a["ffn_gate"],
                                   a["ffn_up"], a["ffn_down"]),
        "w_idx_in": _blocks(w0, slice(960, 964)),
        "w_uk_in": a["even_w_uk"][0].reshape(4, 2, DH, P).transpose(1, 2, 0, 3).reshape(P, 4 * P),
        "w_uv_in": a["even_w_uv"][0].transpose(1, 0, 2).reshape(P, A_HEADS * DH),
        "kv_norm_in": a["even_kv_norm"][0],
        "ln_rows_in": np.stack([np.stack([a[f"ln_{w}_g"][L], a[f"ln_{w}_b"][L]]) for L in range(2)
                                for w in ("mix", "ffn")]),
        "consts_in": constants(),
    }
    arrays["ln_cols_in"] = arrays["ln_rows_in"].reshape(4, 2, KT, P).transpose(3, 0, 1, 2)
    nc = bacc.Bacc("TRN2", target_bir_lowering=False, num_devices=1)
    ap = {}
    for k in arrays:
        arrays[k] = np.ascontiguousarray(arrays[k])
        ap[k] = nc.dram_tensor(k, arrays[k].shape, mybir.dt.from_np(arrays[k].dtype), kind="ExternalInput").ap()
    out = nc.dram_tensor("out_0", (2, P, D), F32, kind="ExternalOutput").ap()
    build(nc, ap["x_in"], ap["xT_in"], ap["stream_in"], ap["w_idx_in"],
          ap["w_uk_in"].rearrange("p (a b) -> p a b", a=4), ap["w_uv_in"].rearrange("p (a b) -> p a b", a=4),
          ap["kv_norm_in"], ap["ln_rows_in"], ap["ln_cols_in"], ap["consts_in"], out)
    r = run_bass_kernel_spmd(nc, [arrays], core_ids=[0])
    return r.results[0]["out_0"].reshape(1, S, D)
```

```python
from contextlib import ExitStack

import concourse.bass as bass
from concourse import mybir

F32 = mybir.dt.float32
F32R = mybir.dt.float32r
ALU = mybir.AluOpType
ACT = mybir.ActivationFunctionType
AX_X = mybir.AxisListType.X

P = 128
D = 1024
S = 256
KT = D // P
DH = 64
A_HEADS, B_HEADS, C_HEADS, I_HEADS = 8, 8, 16, 4
GH = 4
TOPK = min(256, S // 4)
DFF = -(-8 * D // (3 * 256)) * 256
FT = DFF // P
PAIRS = FT // 2
ALPHA = (2 * 2) ** 0.25
LN_EPS, RMS_EPS = 1e-5, 1e-6
CW = 2048
RING, RAW = 6, 2
AHEAD = 4
L0_IN, L0_OUT, L0_FFN = 0, 10, 14
L1_IN = L0_FFN + 3 * PAIRS
L1_OUT = L1_IN + 12
L1_FFN = L1_OUT + 4
CHUNKS = L1_FFN + 3 * PAIRS
NORM_CHUNK = (L0_OUT + 3, L1_IN - 1, L1_OUT + 3, CHUNKS - 1)
NEG = -1e30
MASKED = -1e38
TAKEN = -3e38
TRI = 3 * P


def build(nc, x, xT, stream, w_idx, w_uk, w_uv, kv_norm, ln_rows, ln_cols, consts, out):
    with ExitStack() as ctx:
        def sb(name, shape, dt=F32):
            return ctx.enter_context(nc.sbuf_tensor(name, shape, dt))

        def sem(name):
            return ctx.enter_context(nc.semaphore(name))

        raw = sb("raw", [P, RAW, CW])
        whi = sb("whi", [P, RING, CW], F32R)
        wlo = sb("wlo", [P, RING, CW], F32R)
        h = sb("h", [P, 2, D])
        hThi = sb("hThi", [P, KT, S], F32R)
        hTlo = sb("hTlo", [P, KT, S], F32R)
        oThi = sb("oThi", [P, KT, S], F32R)
        oTlo = sb("oTlo", [P, KT, S], F32R)
        ahi, alo = oThi, oTlo
        qT = sb("qT", [P, KT, S])
        kT = sb("kT", [P, KT, S])
        v = sb("v", [P, 2, D])
        hT = v[:].rearrange("p t (k s) -> p (t k) s", s=S)
        grow = qT[:, 0:4, :].rearrange("p k s -> p (k s)")
        brow = qT[:, 4:8, :].rearrange("p k s -> p (k s)")
        otok = sb("otok", [P, 2, 2 * S])
        prob = sb("prob", [P, 3, TRI])
        probT = sb("probT", [P, 2, TRI])
        scratch = sb("scratch", [P, 5, TRI])
        dist = sb("dist", [P, TRI + 3 * P])
        dsel = sb("dsel", [P, TRI])
        small = sb("small", [P, 192])
        wix = sb("wix", [P, KT, I_HEADS])
        ukv = sb("ukv", [P, 2, 4, P])
        kvrow = sb("kvrow", [P, P])
        zeros = sb("zeros", [P, 512], F32R)
        bank = [ctx.enter_context(nc.psum_tensor(f"bank{b}", [P, 512], F32)) for b in range(8)]

        negtri = dist[:, TRI:TRI + P]
        negones = dist[:, TRI + P:TRI + 2 * P]
        ident = dist[:, TRI + 2 * P:TRI + 3 * P]
        dcaus = dist[:, 0:TRI]
        kiT, cT = kT[:, 4, :], kT[:, 5, :]
        cn = v[:, :, 512:640]
        craw = dsel[:, 0:S].rearrange("p (t c) -> p t c", t=2)
        sgate = scratch[:, 0:2, 0:S]
        aful = scratch[:, 2:4, 0:S]
        idx = scratch[:, 4, :]
        qlT = scratch[:, 0, 0:S]
        olT = scratch[:, 1, 0:S]
        lncol = small[:, 0:64].rearrange("p (n a k) -> p n a k", n=4, a=2)
        wq_i = small[:, 64:72].rearrange("p (t i) -> p t i", t=2)
        m8 = small[:, 72:88].rearrange("p (t e) -> p t e", t=2)
        nmax = small[:, 88:94].rearrange("p (b t) -> p b t", b=3)
        rsum = small[:, 96:112].rearrange("p (b t j) -> p b t j", b=2, t=2)
        rinv = small[:, 112:128].rearrange("p (b t j) -> p b t j", b=2, t=2)
        stats = small[:, 128:152].rearrange("p (t c) -> p t c", t=2)
        mv = small[:, 152:156].rearrange("p (t c) -> p t c", t=2)
        lnv = small[:, 156:158]
        rstd = small[:, 158:160]
        msq = small[:, 160:162]
        eps = small[:, 162:164]

        raw_loaded = [sem(f"raw_loaded{i}") for i in range(RAW)]
        raw_first, whi_first, wlo_first = sem("raw_first"), sem("whi_first"), sem("wlo_first")
        xT_loaded = [sem(f"xT_loaded{i}") for i in range(2)]
        x_loaded, par_loaded, rows_loaded = sem("x_loaded"), sem("par_loaded"), sem("rows_loaded")
        whi_ready, wlo_ready, chunk_used = sem("whi_ready"), sem("wlo_ready"), sem("chunk_used")
        hThi_ready, hTlo_ready, hT_ready = sem("hThi_ready"), sem("hTlo_ready"), sem("hT_ready")
        proj_evac = sem("proj_evac")
        eps_set = sem("eps_set")
        widx_done, widx_ready = sem("widx_done"), sem("widx_ready")
        hT0_ready, hThi0_ready, hTlo0_ready = sem("hT0_ready"), sem("hThi0_ready"), sem("hTlo0_ready")
        msq_ready, clnv_ready, crstd_ready, c_ready, ctr_done, cT_ready = (
            sem("msq_ready"), sem("clnv_ready"), sem("crstd_ready"), sem("c_ready"), sem("ctr_done"), sem("cT_ready"))
        dots_done, relu_done, idx_step, idx_masked, topk_step, dsel_ready = (
            sem("dots_done"), sem("relu_done"), sem("idx_step"), sem("idx_masked"), sem("topk_step"),
            sem("dsel_ready"))
        qlat_done, qlat_ready = sem("qlat_done"), sem("qlat_ready")
        scores_done, logits_done, max_done, probs_ready = (
            sem("scores_done"), sem("logits_done"), sem("max_done"), sem("probs_ready"))
        probT_done, probT_ready, pv_done = sem("probT_done"), sem("probT_ready"), sem("pv_done")
        olat_done, olat_ready = sem("olat_done"), sem("olat_ready")
        rinv_ready, otok_ready, otr_done, oThi_ready, oTlo_ready = (
            sem("rinv_ready"), sem("otok_ready"), sem("otr_done"), sem("oThi_ready"), sem("oTlo_ready"))
        z_done, absz_ready, e_ready, l_ready, sp_ready, sp_masked, rem_done, a_exp, a_masked = (
            sem("z_done"), sem("absz_ready"), sem("e_ready"), sem("l_ready"), sem("sp_ready"), sem("sp_masked"),
            sem("rem_done"), sem("a_exp"), sem("a_masked"))
        acc0_done, res_done, stat_done, mv_ready, lnv_ready, rstd_ready, norm_ready = (
            sem("acc0_done"), sem("res_done"), sem("stat_done"), sem("mv_ready"), sem("lnv_ready"),
            sem("rstd_ready"), sem("norm_ready"))
        tr0_done, tr1_done, scaled, hres_ready = sem("tr0_done"), sem("tr1_done"), sem("scaled"), sem("hres_ready")
        gate_done, silu_ready, amul_ready, ahi_ready, alo_ready = (
            sem("gate_done"), sem("silu_ready"), sem("amul_ready"), sem("ahi_ready"), sem("alo_ready"))
        out_ready, stored = sem("out_ready"), sem("stored")

        block = ctx.enter_context(nc.Block())

        A_UNITS, B_UNITS = A_HEADS + 4, B_HEADS + 2
        A_FILL = {u: (4 + j // 2, j % 2) for j, u in enumerate((0, 1, 2, 3, 4, 5, 6, 8))}
        B_FILL = {m: (8 + m // 2, m % 2) for m in range(B_UNITS)}
        C_START = (0, 1, 2, 4, 5, 7, 8, 10, 11, 13, 14, 16, 17, 18, 19, 20)
        C_AT = {u: hd for hd, u in enumerate(C_START)}
        C_UNITS = 26
        C_FILL = {u: (3 + j // 2, j % 2) for j, u in enumerate([*range(22), 24, 25])}
        C_NORM = {C_START[GH * g + GH - 1] + 3: g for g in range(4)}
        C_TURN = {u + 2: g for u, g in C_NORM.items()}
        LOOPS = (PAIRS - 3) // 2

        @block.sync
        def _(sp):
            HC = CW // 2
            sp.dma_start(hT[:, 0:4], xT[:, 0:4]).then_inc(xT_loaded[0], 16)
            sp.dma_start(raw[:, 0, 0:HC], stream[0][:, 0:HC]).then_inc(raw_first, 16)
            sp.dma_start(hT[:, 4:8], xT[:, 4:8]).then_inc(xT_loaded[1], 16)
            sp.dma_start(raw[:, 0, HC:CW], stream[0][:, HC:CW]).then_inc(raw_loaded[0], 16)
            sp.dma_start(raw[:, 1], stream[1]).then_inc(raw_loaded[1], 16)
            with sp.Fori(1, CHUNKS // RAW) as i:
                for s in range(RAW):
                    sp.wait_ge(wlo_ready, RAW * i + (s + 1 - RAW))
                    sp.dma_start(raw[:, s], stream[RAW * i + s]).then_inc(raw_loaded[s], 16)
            for t in range(2):
                sp.wait_ge(out_ready, t + 1)
                sp.dma_start(out[t], h[:, t]).then_inc(stored, 16)
            sp.wait_ge(stored, 32)

        @block.gpsimd
        def _(pool):
            pool.dma_start(dist[:], consts).then_inc(par_loaded, 16)
            pool.dma_start(wix[:], w_idx).then_inc(par_loaded, 16)
            pool.dma_start(kvrow[:], kv_norm.partition_broadcast(P)).then_inc(par_loaded, 16)
            pool.dma_start(lncol, ln_cols).then_inc(par_loaded, 16)
            pool.dma_start(ukv[:, 0], w_uk).then_inc(par_loaded, 16)
            pool.dma_start(ukv[:, 1], w_uv).then_inc(par_loaded, 16)
            nc.gpsimd.memset(zeros[:].bitcast(F32), 0.0)
            nc.gpsimd.memset(eps[:, 0:1], LN_EPS)
            nc.gpsimd.memset(eps[:, 1:2], RMS_EPS).then_inc(eps_set, 1)

            diag = idx.rearrange("p (b c) -> p b c", b=3)[:, 0:3:2, :]
            pool.wait_ge(idx_step, 2 * I_HEADS)
            nc.gpsimd.affine_select(out=diag, in_=diag, pattern=[[0, 2], [-1, P]], compare_op=ALU.is_ge, fill=NEG,
                                    base=0, channel_multiplier=1).then_inc(idx_masked, 1)
            pool.dma_start(h[:], x).then_inc(x_loaded, 16)

            def zero_future(t, done, n, ready):
                blocks = t.rearrange("p (b c) -> p b c", b=3)[:, 0:3:2, :]
                pool.wait_ge(done, n)
                nc.gpsimd.affine_select(out=blocks, in_=blocks, pattern=[[0, 2], [1, P]], compare_op=ALU.is_gt,
                                        fill=0.0, base=0, channel_multiplier=-1).then_inc(ready, 1)

            for m in range(B_UNITS):
                if m < B_HEADS:
                    zero_future(scratch[:, 2 + m % 3, :], sp_ready, m + 1, sp_masked)
                if 0 <= m - 1 < B_HEADS:
                    zero_future(prob[:, (m - 1) % 3, :], a_exp, m, a_masked)

            for n in range(4):
                if n % 2 == 0:
                    pool.wait_ge(acc0_done, n + 1)
                else:
                    pool.wait_ge(hres_ready, 2 * n)
                pool.dma_start(grow, ln_rows[n, 0].partition_broadcast(P)).then_inc(rows_loaded, 16)
                pool.dma_start(brow, ln_rows[n, 1].partition_broadcast(P)).then_inc(rows_loaded, 16)
                if n < 3:
                    for b in range(4):
                        part = (slice(None), slice(2 * b, 2 * b + 2), slice(0, P))
                        pool.wait_ge(hThi0_ready, 4 * n + b + 1)
                        nc.gpsimd.tensor_tensor(hTlo[part], hT[part], hThi[part].bitcast(F32), ALU.subtract
                                                ).then_inc(hTlo0_ready, 1)
                pool.wait_ge(rows_loaded, 32 * (n + 1))
                for t in range(2 if n < 3 else 1):
                    if n == 3:
                        pool.wait_ge(norm_ready, 7)
                    elif t == 0:
                        pool.wait_ge(tr0_done, n + 1)
                    else:
                        pool.wait_ge(tr1_done, 2 * n + 2)
                    nc.gpsimd.tensor_tensor(h[:, t], h[:, t], grow, ALU.mult).then_inc(scaled, 1)
                    pool.wait_ge(scaled, 2 * n + t + 1)
                    nc.gpsimd.tensor_tensor(h[:, t], h[:, t], brow, ALU.add).then_inc(
                        hres_ready if n < 3 else out_ready, 1)

        @block.scalar
        def _(act):
            def split_hi(c, i=0):
                act.wait_ge(raw_loaded[c % RAW], 16 * (c // RAW + 1) + 16 * (RING // RAW) * i)
                if c >= RING or not isinstance(i, int):
                    act.wait_ge(chunk_used, c - RING + 1 + RING * i)
                nc.scalar.copy(whi[:, c % RING], raw[:, c % RAW]).then_inc(whi_ready, 1)

            def evac_proj(c, n, dst, scale=1.0):
                act.wait_ge(chunk_used, c + 1)
                nc.scalar.activation(dst, bank[4 + n % 2][:].rearrange("p (t c) -> p t c", t=2), ACT.Copy,
                                     scale=scale).then_inc(proj_evac, 1)

            def exp_rows(n, hd):
                act.wait_ge(max_done, 2 * n + 2)
                p = prob[:, n % 3]
                g = hd // GH
                if hd % GH == 0 and n >= 2 * GH:
                    act.wait_ge(rinv_ready, n // GH - 1)
                nc.scalar.activation(p[:, 0:P], p[:, 0:P], ACT.Exp, bias=nmax[:, n % 3, 0:1],
                                     accum_out=rsum[:, g % 2, 0, hd % GH:hd % GH + 1])
                nc.scalar.activation(p[:, P:TRI], p[:, P:TRI], ACT.Exp, bias=nmax[:, n % 3, 1:2],
                                     accum_out=rsum[:, g % 2, 1, hd % GH:hd % GH + 1]).then_inc(probs_ready, 1)

            def evac_probT(n):
                act.wait_ge(probT_done, n + 1)
                if n >= 2:
                    act.wait_ge(pv_done, n - 1)
                nc.scalar.copy(probT[:, n % 2], bank[1][:, 0:TRI]).then_inc(probT_ready, 1)

            def evac_oT_hi(G, kt):
                act.wait_ge(otr_done, G + 1)
                nc.scalar.copy(oThi[:, kt:kt + 2, :], bank[2 + G % 2][:].rearrange("p (k s) -> p k s", k=2)
                               ).then_inc(oThi_ready, 1)

            def norm_rstd(n, t):
                k = 2 * n + t
                act.wait_ge(mv_ready, k + 1)
                nc.scalar.activation(lnv[:, t:t + 1], mv[:, t, 1:2], ACT.Ln, bias=eps[:, 0:1]).then_inc(lnv_ready, 1)
                act.wait_ge(lnv_ready, k + 1)
                nc.scalar.activation(rstd[:, t:t + 1], lnv[:, t:t + 1], ACT.Exp, scale=-0.5).then_inc(rstd_ready, 1)

            def norm(n):
                norm_rstd(n, 0)
                for b in range(4):
                    if b == 1:
                        norm_rstd(n, 1)
                    for k in (2 * b, 2 * b + 1):
                        act.wait_ge(tr0_done, n + 1)
                        nc.scalar.activation(hT[:, k, 0:P], bank[k // 4][:, (k % 4) * P:(k % 4 + 1) * P],
                                             ACT.Identity, scale=lncol[:, n, 0, k:k + 1],
                                             bias=lncol[:, n, 1, k:k + 1]).then_inc(hT0_ready, 1)
                    act.wait_ge(hT0_ready, 8 * n + 2 * b + 2)
                    nc.scalar.copy(hThi[:, 2 * b:2 * b + 2, 0:P], hT[:, 2 * b:2 * b + 2, 0:P]
                                   ).then_inc(hThi0_ready, 1)
                for b in range(4):
                    act.wait_ge(hT_ready, 8 * n + 2 * b + 2)
                    nc.scalar.copy(hThi[:, 2 * b:2 * b + 2, P:S], hT[:, 2 * b:2 * b + 2, P:S]
                                   ).then_inc(hThi_ready, 1)

            act.preload_act_table_set("natural_log_exp_and_others")
            for b in range(4):
                act.wait_ge(xT_loaded[b // 2], 16)
                nc.scalar.copy(hThi[:, 2 * b:2 * b + 2], hT[:, 2 * b:2 * b + 2]).then_inc(hThi_ready, 1)
                if b == 1:
                    act.wait_ge(raw_first, 16)
                    nc.scalar.copy(whi[:, 0, 0:CW // 2], raw[:, 0, 0:CW // 2]).then_inc(whi_first, 1)
            act.wait_ge(raw_loaded[0], 16)
            nc.scalar.copy(whi[:, 0, CW // 2:CW], raw[:, 0, CW // 2:CW]).then_inc(whi_ready, 1)
            for c in range(1, AHEAD):
                split_hi(c)
            act.wait_ge(chunk_used, 1)
            nc.scalar.copy(craw, bank[4][:, S:2 * S].rearrange("p (t c) -> p t c", t=2))
            nc.scalar.copy(kiT, bank[4][:, 0:S]).then_inc(proj_evac, 1)
            act.wait_ge(widx_done, 1)
            nc.scalar.activation(wq_i, bank[6][:, 0:8].rearrange("p (t i) -> p t i", t=2), ACT.Copy,
                                 scale=I_HEADS ** -0.5).then_inc(widx_ready, 1)
            split_hi(4)
            act.wait_ge(eps_set, 1)
            act.wait_ge(msq_ready, 2)
            nc.scalar.activation(lnv, msq, ACT.Ln, bias=eps[:, 1:2], scale=1.0 / P).then_inc(clnv_ready, 1)
            act.wait_ge(clnv_ready, 1)
            nc.scalar.activation(rstd, lnv, ACT.Exp, scale=-0.5).then_inc(crstd_ready, 1)
            evac_proj(1, 1, kT[:, 6:8, :])
            for i in range(I_HEADS):
                act.wait_ge(dots_done, i + 1)
                nc.scalar.activation(scratch[:, i, :], bank[i][:, 0:TRI], ACT.Relu, scale=DH ** -0.5
                                     ).then_inc(relu_done, 1)
            split_hi(5)
            evac_proj(2, 2, qT[:, 4:6, :], DH ** -0.5)
            split_hi(6)
            evac_proj(3, 3, qT[:, 6:8, :], DH ** -0.5)
            split_hi(7)
            act.wait_ge(ctr_done, 1)
            nc.scalar.copy(cT, bank[6][:, 0:S]).then_inc(cT_ready, 1)

            def fill_l0(fill):
                if fill is None:
                    return
                c, half = fill
                if half == 0:
                    split_hi(c + AHEAD)
                elif c < L0_OUT:
                    g, what = (c - 4) // 3, (c - 4) % 3
                    if what == 0:
                        evac_proj(c, c, qT[:, 2 * g:2 * g + 2, :], DH ** -0.5)
                    elif what == 1:
                        evac_proj(c, c, kT[:, 2 * g:2 * g + 2, :])
                    else:
                        evac_proj(c, c, v[:, :, g * S:(g + 1) * S])

            for u in range(12):
                if 0 <= u - 3 < A_HEADS:
                    act.wait_ge(olat_done, u - 2)
                    if u - 3 >= 1:
                        act.wait_ge(pv_done, u - 3)
                    nc.scalar.copy(olT, bank[7][:, 0:S]).then_inc(olat_ready, 1)
                if 0 <= u - 2 < A_HEADS:
                    evac_probT(u - 2)
                if u < A_HEADS:
                    act.wait_ge(qlat_done, u + 1)
                    if u >= 1:
                        act.wait_ge(scores_done, u)
                    if u == 0:
                        act.wait_ge(idx_step, 2 * I_HEADS)
                    nc.scalar.copy(qlT, bank[6][:, 0:S]).then_inc(qlat_ready, 1)
                if 0 <= u - 1 < A_HEADS:
                    exp_rows(u - 1, u - 1)
                fill_l0(A_FILL.get(u))
                if u == 9:
                    evac_oT_hi(0, 0)

            for m in range(B_UNITS):
                if m < B_HEADS:
                    e = scratch[:, m % 2, :]
                    act.wait_ge(z_done, m + 1)
                    if m >= 2:
                        act.wait_ge(sp_ready, m - 1)
                    nc.scalar.activation(e, bank[m % 2][:, 0:TRI], ACT.Abs).then_inc(absz_ready, 1)
                    act.wait_ge(absz_ready, m + 1)
                    nc.scalar.activation(e, e, ACT.Exp, scale=-1.0).then_inc(e_ready, 1)
                    act.wait_ge(e_ready, m + 1)
                    nc.scalar.activation(e, e, ACT.Ln, bias=1.0).then_inc(l_ready, 1)
                if 0 <= m - 1 < B_HEADS:
                    n = m - 1
                    act.wait_ge(rem_done, n + 1)
                    if n >= 3:
                        act.wait_ge(pv_done, A_HEADS + n - 2)
                    nc.scalar.activation(prob[:, n % 3, :], bank[n % 2][:, 0:TRI], ACT.Exp).then_inc(a_exp, 1)
                if m == 1:
                    evac_oT_hi(1, 2)
                if m == 7:
                    evac_oT_hi(2, 4)
                fill_l0(B_FILL[m])
            evac_oT_hi(3, 6)
            split_hi(L0_OUT + 7)

            def ffn_tile(L, c, t, i=0, more=1):
                n = FT * L + t + 4 * i
                act.wait_ge(gate_done, n + 1)
                if t >= 2 or L:
                    act.wait_ge(amul_ready, n - 1)
                nc.scalar.activation(sgate[:, t % 2], bank[2 * (t % 2)][:, 0:S], ACT.Silu).then_inc(silu_ready, 1)
                if more:
                    split_hi(c + AHEAD, i)
                act.wait_ge(amul_ready, n + 1)
                nc.scalar.copy(ahi[:, t % 4, :], aful[:, t % 2]).then_inc(ahi_ready, 1)

            def ffn(L):
                base = L0_FFN if L == 0 else L1_FFN
                for t, at in enumerate((0, 1, 2, 3)):
                    ffn_tile(L, base + at, t)
                with act.Fori(0, LOOPS) as i:
                    for j in range(2):
                        c = base + 4 + 3 * j
                        split_hi(c + AHEAD, i)
                        ffn_tile(L, c + 1, 4 + 2 * j, i)
                        ffn_tile(L, c + 2, 5 + 2 * j, i)
                c = base + 4 + RING * LOOPS
                for at in range(5):
                    more = c + at + AHEAD < CHUNKS
                    if at in (1, 2):
                        ffn_tile(L, c + at, 4 + 4 * LOOPS + at - 1, 0, more)
                    elif more:
                        split_hi(c + at + AHEAD)

            norm(0)
            act.preload_act_table_set("silu_and_others")
            ffn(0)
            act.preload_act_table_set("natural_log_exp_and_others")
            norm(1)

            def evac_l1(q):
                g, what = q // 3, q % 3
                dst = (qT[:, 2 * g:2 * g + 2, :], kT[:, 2 * g:2 * g + 2, :], v[:, :, g * S:(g + 1) * S])[what]
                if q == 0:
                    act.wait_ge(hres_ready, 4)
                evac_proj(L1_IN + q, 10 + q, dst, DH ** -0.5 if what == 0 else 1.0)

            for q in range(3):
                split_hi(L1_IN + q + AHEAD)
                evac_l1(q)
            for u in range(C_UNITS):
                if u - 2 in C_AT:
                    evac_probT(A_HEADS + C_AT[u - 2])
                if u in C_AT:
                    exp_rows(A_HEADS + C_AT[u], C_AT[u])
                if u in C_FILL:
                    q, half = C_FILL[u]
                    if half == 0:
                        split_hi(L1_IN + q + AHEAD)
                    elif q < 12:
                        evac_l1(q)
                if u in C_TURN:
                    evac_oT_hi(4 + C_TURN[u], 2 * C_TURN[u])
            split_hi(L1_OUT + 3 + AHEAD)
            norm(2)
            act.preload_act_table_set("silu_and_others")
            ffn(1)
            act.preload_act_table_set("natural_log_exp_and_others")
            norm_rstd(3, 0)
            norm_rstd(3, 1)

        @block.vector
        def _(dve):
            chained = [0]

            def split_lo(c, i=0):
                dve.wait_ge(whi_ready, c + 1 + RING * i)
                nc.vector.tensor_tensor(wlo[:, c % RING], raw[:, c % RAW], whi[:, c % RING].bitcast(F32),
                                        ALU.subtract).then_inc(wlo_ready, 1)

            def logits(n, slope, table):
                dve.wait_ge(scores_done, n + 1)
                if n >= 3:
                    dve.wait_ge(probT_done, n - 2)
                p = prob[:, n % 3]
                nc.vector.scalar_tensor_tensor(out=p, in0=table, scalar=float(slope), in1=bank[0][:, 0:TRI],
                                               op0=ALU.mult, op1=ALU.add).then_inc(logits_done, 1)
                dve.wait_ge(logits_done, n + 1)
                nc.vector.tensor_reduce(nmax[:, n % 3, 0:1], p[:, 0:P], AX_X, ALU.max, negate=True
                                        ).then_inc(max_done, 1)
                nc.vector.tensor_reduce(nmax[:, n % 3, 1:2], p[:, P:TRI], AX_X, ALU.max, negate=True
                                        ).then_inc(max_done, 1)

            def normalise(G, ng, pvs):
                b = ng % 2
                dve.wait_ge(pv_done, pvs)
                nc.vector.reciprocal(rinv[:, b], rsum[:, b]).then_inc(rinv_ready, 1)
                dve.wait_ge(rinv_ready, ng + 1)
                nc.vector.tensor_tensor(
                    otok[:, G % 2].rearrange("p (a d) -> p a d", d=DH),
                    bank[2 + G % 2][:].rearrange("p (a d) -> p a d", d=DH),
                    rinv[:, b].rearrange("p t j -> p (t j)").unsqueeze(2).to_broadcast([P, 2 * GH, DH]),
                    ALU.mult).then_inc(otok_ready, 1)

            def evac_oT_lo(G, kt):
                dve.wait_ge(oThi_ready, G + 1)
                nc.vector.tensor_tensor(oTlo[:, kt:kt + 2, :], bank[2 + G % 2][:].rearrange("p (k s) -> p k s", k=2),
                                        oThi[:, kt:kt + 2, :].bitcast(F32), ALU.subtract).then_inc(oTlo_ready, 1)

            def norm(n, last=False):
                for t in range(2):
                    k = 2 * n + t
                    if t == 0:
                        dve.wait_ge(acc0_done, n + 1)
                    else:
                        dve.wait_ge(chunk_used, NORM_CHUNK[n] + 1)
                    if n == 0:
                        dve.wait_ge(x_loaded, 16)
                    else:
                        dve.wait_ge(hres_ready, 2 * n)
                    for a in range(2):
                        hh = h[:, t, a * 512:(a + 1) * 512]
                        nc.vector.scalar_tensor_tensor(out=hh, in0=hh, scalar=ALPHA, in1=bank[4 + 2 * t + a][:],
                                                       op0=ALU.mult, op1=ALU.add).then_inc(res_done, 1)
                    for a in range(2):
                        dve.wait_ge(res_done, 2 * k + a + 1)
                        nc.vector.bn_stats(stats[:, t, 6 * a:6 * a + 6], h[:, t, a * 512:(a + 1) * 512]
                                           ).then_inc(stat_done, 1)
                    dve.wait_ge(stat_done, 2 * k + 2)
                    nc.vector.bn_aggr(mv[:, t], stats[:, t]).then_inc(mv_ready, 1)
                    dve.wait_ge(rstd_ready, k + 1)
                    nc.vector.tensor_scalar(h[:, t], h[:, t], mv[:, t, 0:1], rstd[:, t:t + 1], ALU.subtract,
                                            ALU.mult).then_inc(norm_ready, 1)
                if last:
                    return
                def low(b):
                    part = (slice(None), slice(2 * b, 2 * b + 2), slice(P, S))
                    dve.wait_ge(hThi_ready, 4 * (n + 1) + b + 1)
                    nc.vector.tensor_tensor(hTlo[part], hT[part], hThi[part].bitcast(F32), ALU.subtract
                                            ).then_inc(hTlo_ready, 1)

                for k in range(KT):
                    dve.wait_ge(tr1_done, 2 * n + k // 4 + 1)
                    nc.vector.tensor_scalar(hT[:, k, P:S], bank[2 + k // 4][:, (k % 4) * P:(k % 4 + 1) * P],
                                            lncol[:, n, 0, k:k + 1], lncol[:, n, 1, k:k + 1], ALU.mult,
                                            ALU.add).then_inc(hT_ready, 1)
                    if k % 2 == 1 and k >= 3:
                        low(k // 2 - 1)
                low(3)

            for b in range(4):
                dve.wait_ge(hThi_ready, b + 1)
                nc.vector.tensor_tensor(hTlo[:, 2 * b:2 * b + 2], hT[:, 2 * b:2 * b + 2],
                                        hThi[:, 2 * b:2 * b + 2].bitcast(F32), ALU.subtract).then_inc(hTlo_ready, 1)
                if b == 1:
                    dve.wait_ge(whi_first, 1)
                    nc.vector.tensor_tensor(wlo[:, 0, 0:CW // 2], raw[:, 0, 0:CW // 2],
                                            whi[:, 0, 0:CW // 2].bitcast(F32), ALU.subtract).then_inc(wlo_first, 1)
            dve.wait_ge(whi_ready, 1)
            nc.vector.tensor_tensor(wlo[:, 0, CW // 2:CW], raw[:, 0, CW // 2:CW],
                                    whi[:, 0, CW // 2:CW].bitcast(F32), ALU.subtract).then_inc(wlo_ready, 1)
            for c in range(1, AHEAD):
                split_lo(c)
            dve.wait_ge(proj_evac, 1)
            for t in range(2):
                nc.vector.scalar_tensor_tensor(out=prob[:, t, 0:P], in0=craw[:, t], scalar=1.0, in1=craw[:, t],
                                               op0=ALU.mult, op1=ALU.mult, accum_out=msq[:, t:t + 1]
                                               ).then_inc(msq_ready, 1)
            split_lo(4)
            dve.wait_ge(crstd_ready, 1)
            dve.wait_ge(widx_ready, 1)
            dve.wait_ge(par_loaded, 96)
            for t in range(2):
                nc.vector.scalar_tensor_tensor(out=cn[:, t], in0=craw[:, t], scalar=rstd[:, t:t + 1], in1=kvrow[:],
                                               op0=ALU.mult, op1=ALU.mult).then_inc(c_ready, 1)
            cols = (slice(0, P), slice(P, TRI))
            for i in range(I_HEADS):
                dve.wait_ge(relu_done, i + 1)
                for t in range(2):
                    w = wq_i[:, t, i:i + 1]
                    if i == 0:
                        op = nc.vector.tensor_scalar(idx[:, cols[t]], scratch[:, i, cols[t]], w, None, ALU.mult)
                    else:
                        dve.wait_ge(idx_step, 2 * i - 1 + t)
                        op = nc.vector.scalar_tensor_tensor(out=idx[:, cols[t]], in0=scratch[:, i, cols[t]],
                                                            scalar=w, in1=idx[:, cols[t]], op0=ALU.mult,
                                                            op1=ALU.add)
                    op.then_inc(idx_step, 1)
            split_lo(5)
            dve.wait_ge(idx_masked, 1)
            done = 0
            for r in range(TOPK // 8):
                for t in range(2):
                    if r:
                        dve.wait_ge(topk_step, 4 * r - 1 + t)
                    nc.vector.max(m8[:, t], idx[:, cols[t]]).then_inc(topk_step, 1)
                for t in range(2):
                    dve.wait_ge(topk_step, 4 * r + 1 + t)
                    nc.vector.match_replace(idx[:, cols[t]], m8[:, t], idx[:, cols[t]], TAKEN
                                            ).then_inc(topk_step, 1)
                if r in (2, 5):
                    split_lo(6 + r // 3)
            dve.wait_ge(topk_step, 4 * (TOPK // 8))
            nc.vector.tensor_scalar(dsel[:], idx, TAKEN / 1.5, MASKED, ALU.is_gt, ALU.mult).then_inc(dsel_ready, 1)
            dve.wait_ge(dsel_ready, 1)
            nc.vector.tensor_tensor(dsel[:], dsel[:], dcaus, ALU.add).then_inc(dsel_ready, 1)
            dve.wait_ge(dsel_ready, 2)

            for u in range(A_UNITS):
                if 0 <= u - 1 < A_HEADS:
                    logits(u - 1, 2.0 ** (-8.0 * u / A_HEADS), dsel[:])
                if A_FILL.get(u, (0, 1))[1] == 0:
                    split_lo(A_FILL[u][0] + AHEAD)
                if u in (7, 11):
                    normalise(u // 8, u // 8, GH * (u // 8 + 1))
                if u == 9:
                    evac_oT_lo(0, 0)

            for m in range(B_UNITS):
                if m < B_HEADS:
                    e = scratch[:, m % 2, :]
                    dve.wait_ge(l_ready, m + 1)
                    if m >= 3:
                        dve.wait_ge(rem_done, m - 2)
                    nc.vector.scalar_tensor_tensor(out=scratch[:, 2 + m % 3, :], in0=bank[m % 2][:, 0:TRI],
                                                   scalar=0.0, in1=e, op0=ALU.max, op1=ALU.add
                                                   ).then_inc(sp_ready, 1)
                if B_FILL[m][1] == 0:
                    split_lo(B_FILL[m][0] + AHEAD)
                if m == 1:
                    evac_oT_lo(1, 2)
                if m in (5, 9):
                    G = 2 + m // 8
                    dve.wait_ge(pv_done, A_HEADS + m - 1)
                    nc.vector.tensor_copy(otok[:, G % 2], bank[2 + G % 2][:]).then_inc(otok_ready, 1)
                if m == 7:
                    evac_oT_lo(2, 4)
            evac_oT_lo(3, 6)
            split_lo(L0_OUT + 7)

            def ffn_tile(L, c, t, i=0, more=1):
                n = FT * L + t + 4 * i
                dve.wait_ge(silu_ready, n + 1)
                dve.wait_ge(chunk_used, c + 1 + RING * i)
                if t >= 2 or L:
                    dve.wait_ge(alo_ready, n - 1)
                nc.vector.tensor_tensor(aful[:, t % 2], sgate[:, t % 2], bank[2 * (t % 2) + 1][:, 0:S], ALU.mult
                                        ).then_inc(amul_ready, 1)
                if more:
                    split_lo(c + AHEAD, i)
                dve.wait_ge(ahi_ready, n + 1)
                nc.vector.tensor_tensor(alo[:, t % 4, :], aful[:, t % 2], ahi[:, t % 4, :].bitcast(F32),
                                        ALU.subtract).then_inc(alo_ready, 1)

            def ffn(L):
                base = L0_FFN if L == 0 else L1_FFN
                for t, at in enumerate((0, 1, 2, 3)):
                    ffn_tile(L, base + at, t)
                with dve.Fori(0, LOOPS) as i:
                    for j in range(2):
                        c = base + 4 + 3 * j
                        split_lo(c + AHEAD, i)
                        ffn_tile(L, c + 1, 4 + 2 * j, i)
                        ffn_tile(L, c + 2, 5 + 2 * j, i)
                c = base + 4 + RING * LOOPS
                for at in range(5):
                    more = c + at + AHEAD < CHUNKS
                    if at in (1, 2):
                        ffn_tile(L, c + at, 4 + 4 * LOOPS + at - 1, 0, more)
                    elif more:
                        split_lo(c + at + AHEAD)

            norm(0)
            ffn(0)
            norm(1)

            for q in range(3):
                split_lo(L1_IN + q + AHEAD)
            for u in range(C_UNITS):
                if u in C_AT:
                    hd = C_AT[u]
                    logits(A_HEADS + hd, 2.0 ** (-8.0 * (hd + 1) / C_HEADS), dcaus)
                if u in C_NORM:
                    g = C_NORM[u]
                    normalise(4 + g, 2 + g, A_HEADS + B_HEADS + GH * (g + 1))
                if u in C_FILL and C_FILL[u][1] == 0:
                    split_lo(L1_IN + C_FILL[u][0] + AHEAD)
                if u in C_TURN:
                    evac_oT_lo(4 + C_TURN[u], 2 * C_TURN[u])
            split_lo(L1_OUT + 3 + AHEAD)
            norm(2)
            ffn(1)
            norm(3, last=True)
            dve.wait_ge(norm_ready, 8)
            dve.wait_ge(rows_loaded, 128)
            nc.vector.tensor_tensor(h[:, 1], h[:, 1], grow, ALU.mult).then_inc(norm_ready, 1)
            dve.wait_ge(norm_ready, 9)
            dve.wait_ge(out_ready, 1)
            nc.vector.tensor_tensor(h[:, 1], h[:, 1], brow, ALU.add).then_inc(out_ready, 1)

        @block.tensor
        def _(pe):
            mm = nc.tensor.matmul
            HT_PASSES = ((whi, hThi), (whi, hTlo), (wlo, hThi))
            AT_PASSES = ((whi, ahi), (whi, alo), (wlo, ahi))

            def chunk(c, i=0):
                pe.wait_ge(wlo_ready, c + 1 + RING * i)

            def cols_out(dst, slot, off, n=None):
                for k in range(KT):
                    if n is not None and k % 2 == 0:
                        pe.wait_ge(hTlo_ready, 4 * n + k // 2 + 1)
                        if n:
                            pe.wait_ge(hTlo0_ready, 4 * (n - 1) + k // 2 + 1)
                    for j, (w, a) in enumerate(HT_PASSES):
                        last = mm(dst, w[:, slot, off + k * P:off + (k + 1) * P], a[:, k, :],
                                  start=(k == 0 and j == 0), stop=(k == KT - 1 and j == 2))
                return last

            def rows_out(dst, slot, off, t, width):
                for k in range(KT):
                    for j, (w, a) in enumerate(HT_PASSES):
                        last = mm(dst, a[:, k, t * P:(t + 1) * P], w[:, slot, off + k * width:off + (k + 1) * width],
                                  start=(k == 0 and j == 0), stop=(k == KT - 1 and j == 2))
                return last

            def proj_half(c, n, half, is_v, src=None):
                if half == 0:
                    chunk(c)
                    if n >= 2:
                        pe.wait_ge(proj_evac, n - 1)
                dst = bank[4 + n % 2][:, half * S:(half + 1) * S]
                if is_v:
                    last = rows_out(dst, c % RING, 0, half, S)
                else:
                    last = cols_out(dst, c % RING, half * KT * P, src if half == 0 else None)
                if half == 1:
                    last.then_inc(chunk_used, 1)

            def out_tile(c, j, kt, acc_in, start, stop, toks=(0, 1)):
                for t in toks:
                    for a in range(2):
                        for q, (w, o) in enumerate(acc_in):
                            last = mm(bank[4 + 2 * t + a][:], o[:, kt, t * P:(t + 1) * P],
                                      w[:, c % RING, j * D + a * 512:j * D + (a + 1) * 512],
                                      start=(start and q == 0), stop=(stop and q == 2), skip_group_check=True)
                return last

            def last_out(parts, n):
                for t in range(2):
                    for i, (c, kts) in enumerate(parts):
                        for j in range(2):
                            last = out_tile(c, j, kts[j], AT_PASSES, False, j == 1 and i == len(parts) - 1,
                                            toks=(t,))
                        if t == 1:
                            last.then_inc(chunk_used, 1)
                    if t == 0:
                        last.then_inc(acc0_done, 1)

            def transpose_group(G):
                pe.wait_ge(otok_ready, G + 1)
                for k in range(2):
                    for t in range(2):
                        last = nc.tensor.transpose(bank[2 + G % 2][:, k * S + t * P:k * S + (t + 1) * P],
                                                   otok[:, G % 2, t * S + k * P:t * S + (k + 1) * P], ident)
                last.then_inc(otr_done, 1)

            def transpose_probs(n):
                pe.wait_ge(probs_ready, n + 1)
                if n >= 1:
                    pe.wait_ge(probT_ready, n)
                for b in range(3):
                    last = nc.tensor.transpose(bank[1][:, b * P:(b + 1) * P], prob[:, n % 3, b * P:(b + 1) * P],
                                               ident)
                last.then_inc(probT_done, 1)

            def free_group_bank(G):
                if G >= 2:
                    pe.wait_ge(oTlo_ready, G - 1)

            def dots(i):
                p = DH * (i % 2)
                for t in range(2):
                    last = mm(bank[i][:, t * P:t * P + (t + 1) * P], kT[p:p + DH, 6 + i // 2, t * P:(t + 1) * P],
                              kiT[p:p + DH, 0:(t + 1) * P], start=True, stop=True)
                last.then_inc(dots_done, 1)

            pe.wait_ge(wlo_first, 1)
            cols_out(bank[4][:, 0:S], 0, 0, 0)
            chunk(0)
            for t in range(2):
                last = rows_out(bank[4][:, S + t * P:S + (t + 1) * P], 0, KT * P, t, P)
            last.then_inc(chunk_used, 1)
            pe.wait_ge(par_loaded, 96)
            for t in range(2):
                for k in range(KT):
                    last = mm(bank[6][:, t * I_HEADS:(t + 1) * I_HEADS], hT[:, k, t * P:(t + 1) * P], wix[:, k, :],
                              start=(k == 0), stop=(k == KT - 1))
            last.then_inc(widx_done, 1)
            for half in range(2):
                proj_half(1, 1, half, False)
            proj_half(2, 2, 0, False)
            pe.wait_ge(proj_evac, 2)
            for i in range(I_HEADS):
                dots(i)
            proj_half(2, 2, 1, False)
            for half in range(2):
                proj_half(3, 3, half, False)
            pe.wait_ge(c_ready, 2)
            pe.wait_ge(widx_ready, 1)
            for t in range(2):
                last = nc.tensor.transpose(bank[6][:, t * P:(t + 1) * P], cn[:, t], ident)
            last.then_inc(ctr_done, 1)

            def fill_l0(fill):
                if fill is None:
                    return
                c, half = fill
                if c < L0_OUT:
                    proj_half(c, c, half, (c - 4) % 3 == 2)
                else:
                    q = c - L0_OUT
                    if half == 0:
                        chunk(c)
                        pe.wait_ge(oTlo_ready, q + 1)
                        if q == 0:
                            pe.wait_ge(proj_evac, L0_OUT)
                    last = out_tile(c, half, 2 * q + half, AT_PASSES, q == 0 and half == 0, False)
                    if half == 1:
                        last.then_inc(chunk_used, 1)

            pe.wait_ge(relu_done, I_HEADS)
            for u in range(A_UNITS):
                fill_l0(A_FILL.get(u))
                if 0 <= u - 4 < A_HEADS:
                    hd = u - 4
                    pe.wait_ge(olat_ready, hd + 1)
                    if hd % GH == 0:
                        free_group_bank(hd // GH)
                    for t in range(2):
                        at = t * S + (hd % GH) * DH
                        last = mm(bank[2 + hd // GH][:, at:at + DH], olT[:, t * P:(t + 1) * P],
                                  ukv[:, 1].rearrange("p a b -> p (a b)")[:, hd * DH:(hd + 1) * DH], start=True,
                                  stop=True)
                    last.then_inc(pv_done, 1)
                if 0 <= u - 3 < A_HEADS:
                    n = u - 3
                    pe.wait_ge(probT_ready, n + 1)
                    if n >= 1:
                        pe.wait_ge(olat_ready, n)
                    mm(bank[7][:, 0:P], cn[:, 0], probT[:, n % 2, 0:P], start=True, stop=True)
                    mm(bank[7][:, P:S], cn[:, 0], probT[:, n % 2, P:S], start=True, stop=False)
                    mm(bank[7][:, P:S], cn[:, 1], probT[:, n % 2, S:TRI], start=False, stop=True
                       ).then_inc(olat_done, 1)
                if 0 <= u - 2 < A_HEADS:
                    transpose_probs(u - 2)
                if 0 <= u - 1 < A_HEADS:
                    n = u - 1
                    pe.wait_ge(qlat_ready, n + 1)
                    pe.wait_ge(cT_ready, 1)
                    if n >= 1:
                        pe.wait_ge(logits_done, n)
                    for t in range(2):
                        last = mm(bank[0][:, t * P:t * P + (t + 1) * P], qlT[:, t * P:(t + 1) * P],
                                  cT[:, 0:(t + 1) * P], start=True, stop=True)
                    last.then_inc(scores_done, 1)
                if u < A_HEADS:
                    p = DH * (u % 2)
                    if u == 0:
                        pe.wait_ge(proj_evac, 4)
                        pe.wait_ge(cT_ready, 1)
                    else:
                        pe.wait_ge(qlat_ready, u)
                    mm(bank[6][:, 0:S], ukv[p:p + DH, 0].rearrange("p a b -> p (a b)")[:, (u // 2) * P:(u // 2 + 1) * P],
                       qT[p:p + DH, 4 + u // 2, :], start=True, stop=True).then_inc(qlat_done, 1)
                if u == 9:
                    transpose_group(0)

            for m in range(B_UNITS):
                if m < B_HEADS:
                    pe.wait_ge(proj_evac, 6 + 3 * (m // GH))
                    if m >= 2:
                        pe.wait_ge(a_exp, m - 1)
                    p, jt, z = DH * (m % 2), m // 2, bank[m % 2]
                    mm(z[:, 0:S], kT[p:p + DH, jt, 0:P], qT[p:p + DH, jt, :], start=True, stop=False,
                       skip_group_check=True)
                    mm(z[:, S:TRI], kT[p:p + DH, jt, P:S], qT[p:p + DH, jt, P:S], start=False, stop=False,
                       skip_group_check=True).then_inc(z_done, 1)
                if 0 <= m - 2 < B_HEADS:
                    n = m - 2
                    G = 2 + n // GH
                    if n % GH == 0:
                        free_group_bank(G)
                        pe.wait_ge(proj_evac, 7 + 3 * (n // GH))
                    pe.wait_ge(a_masked, n + 1)
                    a = prob[:, n % 3, :]
                    vh = slice(n * DH, (n + 1) * DH)
                    o = bank[2 + G % 2]
                    at = (n % GH) * DH
                    mm(o[:, at:at + DH], a[:, 0:P], v[:, 0, vh], start=True, stop=True)
                    mm(o[:, S + at:S + at + DH], a[:, P:S], v[:, 0, vh], start=True, stop=False)
                    mm(o[:, S + at:S + at + DH], a[:, S:TRI], v[:, 1, vh], start=False, stop=True
                       ).then_inc(pv_done, 1)
                if 0 <= m - 1 < B_HEADS:
                    n = m - 1
                    sp_t = scratch[:, 2 + n % 3, :]
                    z = bank[n % 2]
                    pe.wait_ge(sp_masked, n + 1)
                    mm(z[:, 0:S], negtri, sp_t[:, 0:S], start=False, stop=False, skip_group_check=True)
                    mm(z[:, P:S], negones, sp_t[:, S:TRI], start=False, stop=False, skip_group_check=True)
                    mm(z[:, S:TRI], negtri, sp_t[:, S:TRI], start=False, stop=True, skip_group_check=True
                       ).then_inc(rem_done, 1)
                fill_l0(B_FILL[m])
                if m == 1:
                    transpose_group(1)
                if m == 7:
                    transpose_group(2)
            transpose_group(3)
            chunk(L0_OUT + 3)
            pe.wait_ge(oTlo_ready, 4)
            last_out(((L0_OUT + 3, (6, 7)),), 0)

            def norm_transposes(n, clear):
                for t in range(2):
                    pe.wait_ge(norm_ready, 2 * n + t + 1)
                    for k in range(KT):
                        last = nc.tensor.transpose(bank[2 * t + k // 4][:, (k % 4) * P:(k % 4 + 1) * P],
                                                   h[:, t, k * P:(k + 1) * P], ident)
                        if t == 1 and k % 4 == 3:
                            last.then_inc(tr1_done, 1)
                    if t == 0:
                        last.then_inc(tr0_done, 1)
                    if clear:
                        for b in range(2):
                            mm(bank[4 + 2 * t + b][:], zeros[:, 0:P], zeros[:], start=True, stop=False,
                               skip_group_check=True)

            def gate_up(L, c, t, i=0, src=None):
                n = FT * L + t + 4 * i
                chunk(c, i)
                if t >= 2:
                    pe.wait_ge(amul_ready, n - 1)
                cols_out(bank[2 * (t % 2)][:, 0:S], c % RING, 0, src).then_inc(gate_done, 1)
                cols_out(bank[2 * (t % 2) + 1][:, 0:S], c % RING, KT * P).then_inc(chunk_used, 1)

            def down(L, c, p, i=0):
                chunk(c, i)
                pe.wait_ge(alo_ready, FT * L + 2 * p + 2 + 4 * i)
                for j in range(2):
                    last = out_tile(c, j, (2 * p + j) % 4, AT_PASSES, False, False)
                last.then_inc(chunk_used, 1)

            def ffn(L, n):
                base = L0_FFN if L == 0 else L1_FFN
                norm_transposes(n, True)
                pe.wait_ge(hThi0_ready, 4 * n + 4)
                for t in range(4):
                    gate_up(L, base + t, t, 0, n + 1 if t == 0 else None)
                with pe.Fori(0, LOOPS) as i:
                    for j in range(2):
                        c = base + 4 + 3 * j
                        down(L, c, j, i)
                        gate_up(L, c + 1, 4 + 2 * j, i)
                        gate_up(L, c + 2, 5 + 2 * j, i)
                c, p = base + 4 + RING * LOOPS, 2 * LOOPS
                down(L, c, p)
                gate_up(L, c + 1, 2 * p + 4)
                gate_up(L, c + 2, 2 * p + 5)
                chunk(c + 4)
                pe.wait_ge(alo_ready, FT * (L + 1))
                last_out(((c + 3, ((2 * p + 2) % 4, (2 * p + 3) % 4)), (c + 4, ((2 * p + 4) % 4, (2 * p + 5) % 4))),
                         n + 1)

            ffn(0, 0)

            norm_transposes(1, False)
            for q in range(3):
                for half in range(2):
                    proj_half(L1_IN + q, 10 + q, half, q == 2, 2 if q == 0 else None)
            for u in range(C_UNITS):
                if u in C_TURN and C_TURN[u] == 3:
                    transpose_group(7)
                if u in C_FILL:
                    q, half = C_FILL[u]
                    if q < 12:
                        proj_half(L1_IN + q, 10 + q, half, q % 3 == 2)
                    else:
                        if half == 0:
                            chunk(L1_IN + q)
                            pe.wait_ge(oTlo_ready, 4 + q - 12 + 1)
                            if q == 12:
                                pe.wait_ge(proj_evac, 22)
                        last = out_tile(L1_IN + q, half, 2 * (q - 12) + half, AT_PASSES, q == 12 and half == 0,
                                        False)
                        if half == 1:
                            last.then_inc(chunk_used, 1)
                if u - 3 in C_AT:
                    hd = C_AT[u - 3]
                    n = A_HEADS + hd
                    G = 4 + hd // GH
                    if hd % GH == 0:
                        free_group_bank(G)
                        pe.wait_ge(proj_evac, 10 + 3 * (hd // GH) + 3)
                    pe.wait_ge(probT_ready, n + 1)
                    pt = probT[:, n % 2]
                    vh = slice(hd * DH, (hd + 1) * DH)
                    o = bank[2 + G % 2]
                    at = (hd % GH) * DH
                    mm(o[:, at:at + DH], pt[:, 0:P], v[:, 0, vh], start=True, stop=True)
                    mm(o[:, S + at:S + at + DH], pt[:, P:S], v[:, 0, vh], start=True, stop=False)
                    mm(o[:, S + at:S + at + DH], pt[:, S:TRI], v[:, 1, vh], start=False, stop=True
                       ).then_inc(pv_done, 1)
                if u - 2 in C_AT:
                    transpose_probs(A_HEADS + C_AT[u - 2])
                if u in C_AT:
                    hd = C_AT[u]
                    n = A_HEADS + hd
                    pe.wait_ge(proj_evac, 10 + 3 * (hd // GH) + 2)
                    pe.wait_ge(logits_done, n)
                    p = DH * (hd % 2)
                    for t in range(2):
                        last = mm(bank[0][:, t * P:t * P + (t + 1) * P], qT[p:p + DH, hd // 2, t * P:(t + 1) * P],
                                  kT[p:p + DH, hd // 2, 0:(t + 1) * P], start=True, stop=True)
                    last.then_inc(scores_done, 1)
                if u in C_TURN and C_TURN[u] < 3:
                    transpose_group(4 + C_TURN[u])
            chunk(L1_OUT + 3)
            pe.wait_ge(oTlo_ready, 8)
            last_out(((L1_OUT + 3, (6, 7)),), 2)
            ffn(1, 2)


def _blocks(w, cols):
    return w[:, cols].reshape(KT, P, -1).transpose(1, 0, 2)


def _tiles(w, start, n):
    import numpy as np
    return np.stack([_blocks(w, slice(start + P * j, start + P * (j + 1))) for j in range(n)], 1)


def _rows(w, kt):
    return w[kt * P:(kt + 2) * P].reshape(2, P, -1).transpose(1, 0, 2)


def weight_stream(w_in0, w_out0, w_in1, w_out1, gate, up, down):
    import numpy as np
    ckv, qi, ki, qb = 512, 640, 896, 964
    kb, vb = qb + 512, qb + 1024
    chunks = []

    def add(*parts):
        chunks.append(np.concatenate([p.reshape(P, -1) for p in parts], 1))

    kdup = np.concatenate([w_in0[:, ki:ki + DH]] * 2, 1)
    add(_tiles(kdup, 0, 1), _blocks(w_in0, slice(ckv, ckv + P)))
    add(_tiles(w_in0, qi, 2))
    add(_tiles(w_in0, 0, 2))
    add(_tiles(w_in0, 256, 2))
    for g in range(2):
        add(_tiles(w_in0, qb + S * g, 2))
        add(_tiles(w_in0, kb + S * g, 2))
        add(_blocks(w_in0, slice(vb + S * g, vb + S * (g + 1))))

    def out_rows(w):
        for q in range(4):
            add(_rows(w, 2 * q))

    def ffn(L):
        def gu(t):
            add(_tiles(gate[L], t * P, 1), _tiles(up[L], t * P, 1))
        gu(0)
        gu(1)
        for p in range(1, PAIRS):
            gu(2 * p)
            gu(2 * p + 1)
            add(_rows(down[L], 2 * (p - 1)))
        add(_rows(down[L], 2 * (PAIRS - 1)))

    out_rows(w_out0)
    ffn(0)
    for g in range(4):
        add(_tiles(w_in1, S * g, 2))
        add(_tiles(w_in1, D + S * g, 2))
        add(_blocks(w_in1, slice(2 * D + S * g, 2 * D + S * (g + 1))))
    out_rows(w_out1)
    ffn(1)
    return np.stack(chunks)


def constants():
    import numpy as np
    q = np.arange(P)[:, None]
    k = np.arange(P)[None, :]
    near = np.where(k <= q, k - q, MASKED)
    far = k - (q + P)
    tri = np.where(q >= k, -1.0, 0.0)
    return np.concatenate([near, far, near, tri, -np.ones((P, P)), np.eye(P)], 1).astype(np.float32)


def kernel(**inputs):
    import numpy as np
    import concourse.bacc as bacc
    from concourse.bass_utils import run_bass_kernel_spmd

    a = {k: np.asarray(w) for k, w in inputs.items()}
    xx = a["x"][0]
    w0 = a["even_w_in"][0]
    arrays = {
        "x_in": xx.reshape(2, P, D).transpose(1, 0, 2),
        "xT_in": xx.T.reshape(KT, P, S).transpose(1, 0, 2),
        "stream_in": weight_stream(w0, a["even_w_out"][0], a["odd_w_in"][0], a["odd_w_out"][0], a["ffn_gate"],
                                   a["ffn_up"], a["ffn_down"]),
        "w_idx_in": _blocks(w0, slice(960, 964)),
        "w_uk_in": a["even_w_uk"][0].reshape(4, 2, DH, P).transpose(1, 2, 0, 3).reshape(P, 4 * P),
        "w_uv_in": a["even_w_uv"][0].transpose(1, 0, 2).reshape(P, A_HEADS * DH),
        "kv_norm_in": a["even_kv_norm"][0],
        "ln_rows_in": np.stack([np.stack([a[f"ln_{w}_g"][L], a[f"ln_{w}_b"][L]]) for L in range(2)
                                for w in ("mix", "ffn")]),
        "consts_in": constants(),
    }
    arrays["ln_cols_in"] = arrays["ln_rows_in"].reshape(4, 2, KT, P).transpose(3, 0, 1, 2)
    nc = bacc.Bacc("TRN2", target_bir_lowering=False, num_devices=1)
    ap = {}
    for k in arrays:
        arrays[k] = np.ascontiguousarray(arrays[k])
        ap[k] = nc.dram_tensor(k, arrays[k].shape, mybir.dt.from_np(arrays[k].dtype), kind="ExternalInput").ap()
    out = nc.dram_tensor("out_0", (2, P, D), F32, kind="ExternalOutput").ap()
    build(nc, ap["x_in"], ap["xT_in"], ap["stream_in"], ap["w_idx_in"],
          ap["w_uk_in"].rearrange("p (a b) -> p a b", a=4), ap["w_uv_in"].rearrange("p (a b) -> p a b", a=4),
          ap["kv_norm_in"], ap["ln_rows_in"], ap["ln_cols_in"], ap["consts_in"], out)
    r = run_bass_kernel_spmd(nc, [arrays], core_ids=[0])
    return r.results[0]["out_0"].reshape(1, S, D)
```

```python
from contextlib import ExitStack

import concourse.bass as bass
from concourse import mybir

F32 = mybir.dt.float32
F32R = mybir.dt.float32r
ALU = mybir.AluOpType
ACT = mybir.ActivationFunctionType
AX_X = mybir.AxisListType.X

P = 128
D = 1024
S = 256
KT = D // P
DH = 64
A_HEADS, B_HEADS, C_HEADS, I_HEADS = 8, 8, 16, 4
GH = 4
TOPK = min(256, S // 4)
DFF = -(-8 * D // (3 * 256)) * 256
FT = DFF // P
PAIRS = FT // 2
ALPHA = (2 * 2) ** 0.25
LN_EPS, RMS_EPS = 1e-5, 1e-6
CW = 2048
HW = CW // 2
RING, RAW = 6, 2
AHEAD = 4
L0_IN, L0_OUT, L0_FFN = 0, 10, 14
L1_IN = L0_FFN + 3 * PAIRS
L1_OUT = L1_IN + 12
L1_FFN = L1_OUT + 4
CHUNKS = L1_FFN + 3 * PAIRS
NORM_CHUNK = (L0_OUT + 3, L1_IN - 1, L1_OUT + 3, CHUNKS - 1)
NEG = -1e30
MASKED = -1e38
TAKEN = -3e38
TRI = 3 * P


def build(nc, x, xT, stream, w_uk, w_uv, kv_norm, ln_rows, consts, out):
    with ExitStack() as ctx:
        def sb(name, shape, dt=F32):
            return ctx.enter_context(nc.sbuf_tensor(name, shape, dt))

        def sem(name):
            return ctx.enter_context(nc.semaphore(name))

        raw = sb("raw", [P, RAW, CW])
        whi = sb("whi", [P, RING, CW], F32R)
        wlo = sb("wlo", [P, RING, CW], F32R)
        h = sb("h", [P, 2, D])
        hThi = sb("hThi", [P, KT, S], F32R)
        hTlo = sb("hTlo", [P, KT, S], F32R)
        oThi = sb("oThi", [P, KT, S], F32R)
        oTlo = sb("oTlo", [P, KT, S], F32R)
        ahi, alo = oThi, oTlo
        qT = sb("qT", [P, KT, S])
        kT = sb("kT", [P, KT, S])
        v = sb("v", [P, 2, D])
        hT = v[:].rearrange("p t (k s) -> p (t k) s", s=S)
        grow = qT[:, 0:4, :].rearrange("p k s -> p (k s)")
        brow = qT[:, 4:8, :].rearrange("p k s -> p (k s)")
        otok = sb("otok", [P, 2, 2 * S])
        prob = sb("prob", [P, 3, TRI])
        probT = sb("probT", [P, 2, TRI])
        scratch = sb("scratch", [P, 5, TRI])
        dist = sb("dist", [P, TRI + 3 * P])
        dsel = sb("dsel", [P, TRI])
        small = sb("small", [P, 192])
        ukv = sb("ukv", [P, 2, 4, P])
        kvrow = sb("kvrow", [P, P])
        zeros = sb("zeros", [P, 512], F32R)
        bank = [ctx.enter_context(nc.psum_tensor(f"bank{b}", [P, 512], F32)) for b in range(8)]

        negtri = dist[:, TRI:TRI + P]
        negones = dist[:, TRI + P:TRI + 2 * P]
        ident = dist[:, TRI + 2 * P:TRI + 3 * P]
        dcaus = dist[:, 0:TRI]
        wT = otok[DH:DH + I_HEADS, 0, 0:S]
        kiT, cT = kT[:, 4, :], kT[:, 5, :]
        cn = v[:, :, 512:640]
        crawT = dsel[:, 0:S]
        craw = bank[7][:, 0:S].rearrange("p (t c) -> p t c", t=2)
        sgate = scratch[:, 0:2, 0:S]
        aful = scratch[:, 2:4, 0:S]
        idx = scratch[:, 4, :]
        qlT = scratch[:, 0, 0:S]
        olT = scratch[:, 1, 0:S]
        wq_i = small[:, 64:72].rearrange("p (t i) -> p t i", t=2)
        m8 = small[:, 72:88].rearrange("p (t e) -> p t e", t=2)
        nmax = small[:, 88:94].rearrange("p (b t) -> p b t", b=3)
        rsum = small[:, 96:112].rearrange("p (b t j) -> p b t j", b=2, t=2)
        rinv = small[:, 112:128].rearrange("p (b t j) -> p b t j", b=2, t=2)
        stats = small[:, 128:152].rearrange("p (t c) -> p t c", t=2)
        mv = small[:, 152:156].rearrange("p (t c) -> p t c", t=2)
        lnv = small[:, 156:158]
        rstd = small[:, 158:160]
        msq = small[:, 160:162]
        eps = small[:, 162:164]

        raw_loaded = [[sem(f"raw_loaded{i}{j}") for j in range(2)] for i in range(RAW)]
        xT_loaded = [sem(f"xT_loaded{i}") for i in range(2)]
        dist_loaded = sem("dist_loaded")
        x_loaded, par_loaded, rows_loaded = sem("x_loaded"), sem("par_loaded"), sem("rows_loaded")
        whi_ready, wlo_ready, chunk_used = sem("whi_ready"), sem("wlo_ready"), sem("chunk_used")
        hThi_ready, hTlo_ready = sem("hThi_ready"), sem("hTlo_ready")
        proj_evac = sem("proj_evac")
        eps_set = sem("eps_set")
        widx_done, widx_ready = sem("widx_done"), sem("widx_ready")
        hThi0_ready, hTlo0_ready = sem("hThi0_ready"), sem("hTlo0_ready")
        craw_done, ff_turned = sem("craw_done"), sem("ff_turned")
        msq_ready, clnv_ready, crstd_ready, c_ready, ctr_done, cT_ready = (
            sem("msq_ready"), sem("clnv_ready"), sem("crstd_ready"), sem("c_ready"), sem("ctr_done"), sem("cT_ready"))
        dots_done, relu_done, idx_step, idx_masked, topk_step, dsel_ready = (
            sem("dots_done"), sem("relu_done"), sem("idx_step"), sem("idx_masked"), sem("topk_step"),
            sem("dsel_ready"))
        qlat_done, qlat_ready = sem("qlat_done"), sem("qlat_ready")
        scores_done, logits_done, max_done, probs_ready = (
            sem("scores_done"), sem("logits_done"), sem("max_done"), sem("probs_ready"))
        probT_done, probT_ready, pv_done = sem("probT_done"), sem("probT_ready"), sem("pv_done")
        olat_done, olat_ready = sem("olat_done"), sem("olat_ready")
        rinv_ready, otok_ready, otr_done, oThi_ready, oTlo_ready = (
            sem("rinv_ready"), sem("otok_ready"), sem("otr_done"), sem("oThi_ready"), sem("oTlo_ready"))
        z_done, absz_ready, e_ready, l_ready, sp_ready, sp_masked, rem_done, a_exp, a_masked = (
            sem("z_done"), sem("absz_ready"), sem("e_ready"), sem("l_ready"), sem("sp_ready"), sem("sp_masked"),
            sem("rem_done"), sem("a_exp"), sem("a_masked"))
        acc_done, res_done, stat_done, mv_ready, lnv_ready, rstd_ready, norm_ready = (
            sem("acc_done"), sem("res_done"), sem("stat_done"), sem("mv_ready"), sem("lnv_ready"),
            sem("rstd_ready"), sem("norm_ready"))
        tr0_done, tr1_done, scaled = sem("tr0_done"), sem("tr1_done"), sem("scaled")
        gate_done, silu_ready, amul_ready, ahi_ready, alo_ready = (
            sem("gate_done"), sem("silu_ready"), sem("amul_ready"), sem("ahi_ready"), sem("alo_ready"))
        stored = sem("stored")

        block = ctx.enter_context(nc.Block())

        A_UNITS, B_UNITS = A_HEADS + 4, B_HEADS + 2
        A_FILL = {u: (4 + j // 2, j % 2) for j, u in enumerate((0, 1, 2, 3, 4, 5, 6, 8))}
        B_FILL = {m: (8 + m // 2, m % 2) for m in range(B_UNITS)}
        C_START = (0, 1, 2, 4, 5, 7, 8, 10, 11, 13, 14, 16, 17, 18, 19, 20)
        C_AT = {u: hd for hd, u in enumerate(C_START)}
        C_UNITS = 26
        C_FILL = {u: (3 + j // 2, j % 2) for j, u in enumerate([*range(22), 24, 25])}
        C_NORM = {C_START[GH * g + GH - 1] + 3: g for g in range(4)}
        C_TURN = {u + 2: g for u, g in C_NORM.items()}
        LOOPS = (PAIRS - 3) // 2
        FF_SLOT = [t % 4 for t in range(FT - 2)] + [4, 5]
        TR_BANK = (4, 0, 4)

        def turned_groups(G):
            return G + 1 if G < 2 else G - 1

        def tr_bank(n, t, a):
            return bank[TR_BANK[n] + 2 * t + a][:].rearrange("p (k s) -> p k s", k=4)

        def rows_bank(t):
            return bank[2 * t][:].rearrange("p (t f) -> p t f", t=2)


        @block.sync
        def _(sp):
            half = (slice(0, HW), slice(HW, CW))
            sp.dma_start(raw[:, 0, half[0]], stream[0][:, half[0]]).then_inc(raw_loaded[0][0], 16)
            for j in range(2):
                sp.dma_start(hT[:, 4 * j:4 * j + 4], xT[:, 4 * j:4 * j + 4]).then_inc(xT_loaded[j], 16)
            sp.dma_start(raw[:, 0, half[1]], stream[0][:, half[1]]).then_inc(raw_loaded[0][1], 16)
            for j in range(2):
                sp.dma_start(raw[:, 1, half[j]], stream[1][:, half[j]]).then_inc(raw_loaded[1][j], 16)
            with sp.Fori(1, CHUNKS // RAW) as i:
                for s in range(RAW):
                    for j in range(2):
                        sp.wait_ge(wlo_ready, 2 * RAW * i + (2 * (s - RAW) + j + 1))
                        sp.dma_start(raw[:, s, half[j]], stream[RAW * i + s][:, half[j]]
                                     ).then_inc(raw_loaded[s][j], 16)
            for t in range(2):
                for a in range(2):
                    cols = slice(a * 512, (a + 1) * 512)
                    sp.wait_ge(norm_ready, 12 + 2 * t + a + 1)
                    sp.dma_start(out[t][:, cols], h[:, t, cols]).then_inc(stored, 16)
            sp.wait_ge(stored, 64)

        @block.gpsimd
        def _(pool):
            nc.gpsimd.memset(zeros[:].bitcast(F32), 0.0)
            nc.gpsimd.memset(eps[:, 0:1], LN_EPS)
            nc.gpsimd.memset(eps[:, 1:2], RMS_EPS).then_inc(eps_set, 1)
            pool.wait_ge(raw_loaded[0][0], 16)
            pool.dma_start(dist[:], consts).then_inc(dist_loaded, 16)
            pool.dma_start(kvrow[:], kv_norm.partition_broadcast(P)).then_inc(par_loaded, 16)
            pool.dma_start(ukv[:, 0], w_uk).then_inc(par_loaded, 16)
            pool.dma_start(ukv[:, 1], w_uv).then_inc(par_loaded, 16)

            diag = idx.rearrange("p (b c) -> p b c", b=3)[:, 0:3:2, :]
            pool.wait_ge(idx_step, 2 * I_HEADS)
            nc.gpsimd.affine_select(out=diag, in_=diag, pattern=[[0, 2], [-1, P]], compare_op=ALU.is_ge, fill=NEG,
                                    base=0, channel_multiplier=1).then_inc(idx_masked, 1)
            pool.dma_start(h[:], x).then_inc(x_loaded, 16)

            def zero_future(t, done, n, ready):
                blocks = t.rearrange("p (b c) -> p b c", b=3)[:, 0:3:2, :]
                pool.wait_ge(done, n)
                nc.gpsimd.affine_select(out=blocks, in_=blocks, pattern=[[0, 2], [1, P]], compare_op=ALU.is_gt,
                                        fill=0.0, base=0, channel_multiplier=-1).then_inc(ready, 1)

            for m in range(B_UNITS):
                if m < B_HEADS:
                    zero_future(scratch[:, 2 + m % 3, :], sp_ready, m + 1, sp_masked)
                if 0 <= m - 1 < B_HEADS:
                    zero_future(prob[:, (m - 1) % 3, :], a_exp, m, a_masked)

            for n in range(4):
                if n % 2 == 0:
                    pool.wait_ge(z_done if n == 0 else scores_done, B_HEADS if n == 0 else A_HEADS + C_HEADS)
                else:
                    pool.wait_ge(norm_ready, 4 * n)
                pool.dma_start(grow, ln_rows[n, 0].partition_broadcast(P)).then_inc(rows_loaded, 16)
                pool.dma_start(brow, ln_rows[n, 1].partition_broadcast(P)).then_inc(rows_loaded, 16)
                if n < 3:
                    for b in range(4):
                        part = (slice(None), slice(2 * b, 2 * b + 2), slice(0, P))
                        pool.wait_ge(hThi0_ready, 4 * n + b + 1)
                        nc.gpsimd.tensor_tensor(hTlo[part], hT[part], hThi[part].bitcast(F32), ALU.subtract
                                                ).then_inc(hTlo0_ready, 1)

        @block.scalar
        def _(act):
            def split_hi_half(c, j, i=0):
                act.wait_ge(raw_loaded[c % RAW][j], 16 * (c // RAW + 1) + 16 * (RING // RAW) * i)
                nc.scalar.copy(whi[:, c % RING, j * HW:(j + 1) * HW], raw[:, c % RAW, j * HW:(j + 1) * HW]
                               ).then_inc(whi_ready, 1)

            def split_hi(c, i=0):
                if c >= RING or not isinstance(i, int):
                    act.wait_ge(chunk_used, c - RING + 1 + RING * i)
                for j in range(2):
                    split_hi_half(c, j, i)

            def evac_proj(c, n, dst, scale=1.0):
                act.wait_ge(chunk_used, c + 1)
                nc.scalar.activation(dst, bank[4 + n % 2][:].rearrange("p (t c) -> p t c", t=2), ACT.Copy,
                                     scale=scale).then_inc(proj_evac, 1)

            def exp_rows(n, hd):
                act.wait_ge(max_done, 2 * n + 2)
                p = prob[:, n % 3]
                g = hd // GH
                if hd % GH == 0 and n >= 2 * GH:
                    act.wait_ge(rinv_ready, n // GH - 1)
                nc.scalar.activation(p[:, 0:P], p[:, 0:P], ACT.Exp, bias=nmax[:, n % 3, 0:1],
                                     accum_out=rsum[:, g % 2, 0, hd % GH:hd % GH + 1])
                nc.scalar.activation(p[:, P:TRI], p[:, P:TRI], ACT.Exp, bias=nmax[:, n % 3, 1:2],
                                     accum_out=rsum[:, g % 2, 1, hd % GH:hd % GH + 1]).then_inc(probs_ready, 1)

            def evac_probT(n):
                act.wait_ge(probT_done, n + 1)
                if n >= 2:
                    act.wait_ge(pv_done, n - 1)
                nc.scalar.copy(probT[:, n % 2], bank[1][:, 0:TRI]).then_inc(probT_ready, 1)

            def evac_oT_hi(G, kt):
                if G in (2, 3):
                    act.wait_ge(pv_done, A_HEADS + GH * (G - 1))
                else:
                    act.wait_ge(otr_done, turned_groups(G))
                nc.scalar.copy(oThi[:, kt:kt + 2, :], bank[2 + G % 2][:].rearrange("p (k s) -> p k s", k=2)
                               ).then_inc(oThi_ready, 1)

            def norm_rstd(n, t):
                k = 2 * n + t
                act.wait_ge(mv_ready, k + 1)
                nc.scalar.activation(lnv[:, t:t + 1], mv[:, t, 1:2], ACT.Ln, bias=eps[:, 0:1]).then_inc(lnv_ready, 1)
                act.wait_ge(lnv_ready, k + 1)
                nc.scalar.activation(rstd[:, t:t + 1], lnv[:, t:t + 1], ACT.Exp, scale=-0.5).then_inc(rstd_ready, 1)

            def norm(n):
                norm_rstd(n, 0)
                for b in range(4):
                    part = (slice(None), slice(2 * b, 2 * b + 2), slice(0, P))
                    turned = tr_bank(n, 0, b // 2)[:, 2 * (b % 2):2 * (b % 2) + 2, :]
                    act.wait_ge(tr0_done, 2 * n + b // 2 + 1)
                    nc.scalar.copy(hT[part], turned)
                    nc.scalar.copy(hThi[part], turned).then_inc(hThi0_ready, 1)
                norm_rstd(n, 1)
                split_hi(NORM_CHUNK[n] + AHEAD)
                for a in range(2):
                    act.wait_ge(tr1_done, 2 * n + a + 1)
                    nc.scalar.copy(hThi[:, 4 * a:4 * a + 4, P:S], tr_bank(n, 1, a)).then_inc(hThi_ready, 1)

            act.preload_act_table_set("natural_log_exp_and_others")
            split_hi_half(0, 0)
            for b in range(4):
                act.wait_ge(xT_loaded[b // 2], 16)
                nc.scalar.copy(hThi[:, 2 * b:2 * b + 2], hT[:, 2 * b:2 * b + 2]).then_inc(hThi_ready, 1)
            split_hi_half(0, 1)
            for c in (1, 2):
                split_hi(c)
            act.wait_ge(chunk_used, 1)
            nc.scalar.copy(crawT, bank[4][:, S:2 * S])
            nc.scalar.copy(wT, bank[4][DH:DH + I_HEADS, 0:S])
            nc.scalar.copy(kiT[0:DH], bank[4][0:DH, 0:S])
            nc.scalar.copy(kiT[DH:P], bank[4][0:DH, 0:S]).then_inc(proj_evac, 1)
            split_hi(3)
            evac_proj(1, 1, kT[:, 6:8, :])
            act.wait_ge(widx_done, 1)
            nc.scalar.activation(wq_i, bank[6][:, 0:8].rearrange("p (t i) -> p t i", t=2), ACT.Copy,
                                 scale=I_HEADS ** -0.5).then_inc(widx_ready, 1)
            for i in range(I_HEADS):
                act.wait_ge(dots_done, i + 1)
                nc.scalar.activation(scratch[:, i, :], bank[i][:, 0:TRI], ACT.Relu, scale=DH ** -0.5
                                     ).then_inc(relu_done, 1)
            split_hi(4)
            act.wait_ge(eps_set, 1)
            act.wait_ge(craw_done, 1)
            for t in range(2):
                nc.scalar.activation(prob[:, t, 0:P], craw[:, t], ACT.Square, accum_out=msq[:, t:t + 1]
                                     ).then_inc(msq_ready, 1)
            act.wait_ge(msq_ready, 2)
            nc.scalar.activation(lnv, msq, ACT.Ln, bias=eps[:, 1:2], scale=1.0 / P).then_inc(clnv_ready, 1)
            act.wait_ge(clnv_ready, 1)
            nc.scalar.activation(rstd, lnv, ACT.Exp, scale=-0.5).then_inc(crstd_ready, 1)
            split_hi(5)
            evac_proj(2, 2, qT[:, 4:6, :], DH ** -0.5)
            split_hi(6)
            evac_proj(3, 3, qT[:, 6:8, :], DH ** -0.5)
            split_hi(7)
            act.wait_ge(ctr_done, 1)
            nc.scalar.copy(cT, bank[6][:, 0:S]).then_inc(cT_ready, 1)

            def fill_l0(fill):
                if fill is None:
                    return
                c, half = fill
                if half == 0:
                    split_hi(c + AHEAD)
                elif c < L0_OUT:
                    g, what = (c - 4) // 3, (c - 4) % 3
                    if what == 0:
                        evac_proj(c, c, qT[:, 2 * g:2 * g + 2, :], DH ** -0.5)
                    elif what == 1:
                        evac_proj(c, c, kT[:, 2 * g:2 * g + 2, :])
                    else:
                        evac_proj(c, c, v[:, :, g * S:(g + 1) * S])

            for u in range(12):
                if A_FILL.get(u, (0, 0))[1] == 1:
                    fill_l0(A_FILL[u])
                if 0 <= u - 3 < A_HEADS:
                    act.wait_ge(olat_done, u - 2)
                    if u - 3 >= 1:
                        act.wait_ge(pv_done, u - 3)
                    nc.scalar.copy(olT, bank[7][:, 0:S]).then_inc(olat_ready, 1)
                if 0 <= u - 2 < A_HEADS:
                    evac_probT(u - 2)
                if u < A_HEADS:
                    act.wait_ge(qlat_done, u + 1)
                    if u >= 1:
                        act.wait_ge(scores_done, u)
                    if u == 0:
                        act.wait_ge(idx_step, 2 * I_HEADS)
                    nc.scalar.copy(qlT, bank[6][:, 0:S]).then_inc(qlat_ready, 1)
                if 0 <= u - 1 < A_HEADS:
                    exp_rows(u - 1, u - 1)
                if A_FILL.get(u, (0, 1))[1] == 0:
                    fill_l0(A_FILL[u])
                if u == 9:
                    evac_oT_hi(0, 0)

            for m in range(B_UNITS):
                if m < B_HEADS:
                    e = scratch[:, m % 2, :]
                    act.wait_ge(z_done, m + 1)
                    if m >= 2:
                        act.wait_ge(sp_ready, m - 1)
                    nc.scalar.activation(e, bank[m % 2][:, 0:TRI], ACT.Abs).then_inc(absz_ready, 1)
                    act.wait_ge(absz_ready, m + 1)
                    nc.scalar.activation(e, e, ACT.Exp, scale=-1.0).then_inc(e_ready, 1)
                    act.wait_ge(e_ready, m + 1)
                    nc.scalar.activation(e, e, ACT.Ln, bias=1.0).then_inc(l_ready, 1)
                if 0 <= m - 1 < B_HEADS:
                    n = m - 1
                    act.wait_ge(rem_done, n + 1)
                    if n >= 3:
                        act.wait_ge(pv_done, A_HEADS + n - 2)
                    nc.scalar.activation(prob[:, n % 3, :], bank[n % 2][:, 0:TRI], ACT.Exp).then_inc(a_exp, 1)
                if m == 1:
                    evac_oT_hi(1, 2)
                if m == 6:
                    evac_oT_hi(2, 4)
                fill_l0(B_FILL[m])
            evac_oT_hi(3, 6)

            def ffn_rows(L, base):
                split_hi(base + 4)
                for t in range(2):
                    n = FT * L + t
                    act.wait_ge(chunk_used, base + t + 1)
                    if L:
                        act.wait_ge(amul_ready, n - 1)
                    nc.scalar.activation(sgate[:, t].rearrange("p (t f) -> p t f", t=2), rows_bank(t)[:, :, 0:P],
                                         ACT.Silu).then_inc(silu_ready, 1)
                for t in range(2):
                    act.wait_ge(ff_turned, 2 * L + t + 1)
                    nc.scalar.copy(ahi[:, t, :], bank[2 * t + 1][:, 0:S]).then_inc(ahi_ready, 1)
                split_hi(base + 5)

            def ffn_tile(L, c, t, i=0, more=1, ahi_first=False):
                n = FT * L + t + 4 * i
                act.wait_ge(gate_done, n + 1 - 2 * (L + 1))
                act.wait_ge(amul_ready, n - 1)
                nc.scalar.activation(sgate[:, t % 2], bank[2 * (t % 2)][:, 0:S], ACT.Silu).then_inc(silu_ready, 1)
                if more and not ahi_first:
                    split_hi(c + AHEAD, i)
                act.wait_ge(amul_ready, n + 1)
                nc.scalar.copy(ahi[:, FF_SLOT[t], :], aful[:, t % 2]).then_inc(ahi_ready, 1)
                if more and ahi_first:
                    split_hi(c + AHEAD, i)

            def ffn(L):
                base = L0_FFN if L == 0 else L1_FFN
                ffn_rows(L, base)
                for t in (2, 3):
                    ffn_tile(L, base + t, t)
                with act.Fori(0, LOOPS) as i:
                    for j in range(2):
                        c = base + 4 + 3 * j
                        split_hi(c + AHEAD, i)
                        ffn_tile(L, c + 1, 4 + 2 * j, i)
                        ffn_tile(L, c + 2, 5 + 2 * j, i)
                c = base + 4 + RING * LOOPS
                for at in range(4):
                    more = c + at + AHEAD < CHUNKS
                    if at < 2:
                        ffn_tile(L, c + at, 4 + 4 * LOOPS + at, 0, more, at == 1)
                    elif more:
                        split_hi(c + at + AHEAD)

            norm(0)
            act.preload_act_table_set("silu_and_others")
            ffn(0)
            act.preload_act_table_set("natural_log_exp_and_others")
            norm(1)

            def evac_l1(q):
                g, what = q // 3, (q + 2 * (q < 3)) % 3
                dst = (qT[:, 2 * g:2 * g + 2, :], kT[:, 2 * g:2 * g + 2, :], v[:, :, g * S:(g + 1) * S])[what]
                if q == 1:
                    act.wait_ge(norm_ready, 8)
                evac_proj(L1_IN + q, 10 + q, dst, DH ** -0.5 if what == 0 else 1.0)

            for q in range(3):
                split_hi(L1_IN + q + AHEAD)
                evac_l1(q)
            for u in range(C_UNITS):
                if u - 2 in C_AT:
                    evac_probT(A_HEADS + C_AT[u - 2])
                q, half = C_FILL.get(u, (12, 1))
                if half == 1 and q < 12:
                    evac_l1(q)
                if u in C_AT:
                    exp_rows(A_HEADS + C_AT[u], C_AT[u])
                if half == 0:
                    split_hi(L1_IN + q + AHEAD)
                if u in C_TURN:
                    evac_oT_hi(4 + C_TURN[u], 2 * C_TURN[u])
            norm(2)
            act.preload_act_table_set("silu_and_others")
            ffn(1)
            act.preload_act_table_set("natural_log_exp_and_others")
            norm_rstd(3, 0)
            norm_rstd(3, 1)

        @block.vector
        def _(dve):
            def split_lo_half(c, j, i=0):
                cols = slice(j * HW, (j + 1) * HW)
                dve.wait_ge(whi_ready, 2 * c + j + 1 + 2 * RING * i)
                nc.vector.tensor_tensor(wlo[:, c % RING, cols], raw[:, c % RAW, cols],
                                        whi[:, c % RING, cols].bitcast(F32), ALU.subtract).then_inc(wlo_ready, 1)

            def split_lo(c, i=0):
                for j in range(2):
                    split_lo_half(c, j, i)

            def logits(n, slope, table):
                dve.wait_ge(scores_done, n + 1)
                if n >= 3:
                    dve.wait_ge(probT_done, n - 2)
                p = prob[:, n % 3]
                nc.vector.scalar_tensor_tensor(out=p, in0=table, scalar=float(slope), in1=bank[0][:, 0:TRI],
                                               op0=ALU.mult, op1=ALU.add).then_inc(logits_done, 1)
                dve.wait_ge(logits_done, n + 1)
                nc.vector.tensor_reduce(nmax[:, n % 3, 0:1], p[:, 0:P], AX_X, ALU.max, negate=True
                                        ).then_inc(max_done, 1)
                nc.vector.tensor_reduce(nmax[:, n % 3, 1:2], p[:, P:TRI], AX_X, ALU.max, negate=True
                                        ).then_inc(max_done, 1)

            def normalise(G, ng, pvs):
                b = ng % 2
                dve.wait_ge(pv_done, pvs)
                nc.vector.reciprocal(rinv[:, b], rsum[:, b]).then_inc(rinv_ready, 1)
                dve.wait_ge(rinv_ready, ng + 1)
                nc.vector.tensor_tensor(
                    otok[:, G % 2].rearrange("p (a d) -> p a d", d=DH),
                    bank[2 + G % 2][:].rearrange("p (a d) -> p a d", d=DH),
                    rinv[:, b].rearrange("p t j -> p (t j)").unsqueeze(2).to_broadcast([P, 2 * GH, DH]),
                    ALU.mult).then_inc(otok_ready, 1)

            def evac_oT_lo(G, kt):
                dve.wait_ge(oThi_ready, G + 1)
                nc.vector.tensor_tensor(oTlo[:, kt:kt + 2, :], bank[2 + G % 2][:].rearrange("p (k s) -> p k s", k=2),
                                        oThi[:, kt:kt + 2, :].bitcast(F32), ALU.subtract).then_inc(oTlo_ready, 1)

            def norm(n):
                last = n == 3
                if n == 0:
                    dve.wait_ge(x_loaded, 16)
                for t in range(2):
                    k = 2 * n + t
                    for a in range(2):
                        hh = h[:, t, a * 512:(a + 1) * 512]
                        if t and a:
                            dve.wait_ge(chunk_used, NORM_CHUNK[n] + 1)
                        else:
                            dve.wait_ge(acc_done, 3 * n + 2 * t + a + 1)
                        nc.vector.scalar_tensor_tensor(out=hh, in0=hh, scalar=ALPHA, in1=bank[4 + 2 * t + a][:],
                                                       op0=ALU.mult, op1=ALU.add).then_inc(res_done, 1)
                        dve.wait_ge(res_done, 2 * k + a + 1)
                        nc.vector.bn_stats(stats[:, t, 6 * a:6 * a + 6], hh).then_inc(stat_done, 1)
                    dve.wait_ge(stat_done, 2 * k + 2)
                    nc.vector.bn_aggr(mv[:, t], stats[:, t]).then_inc(mv_ready, 1)
                    dve.wait_ge(mv_ready, k + 1)
                    dve.wait_ge(rows_loaded, 32 * (n + 1))
                    for a in range(2):
                        cols = slice(a * 512, (a + 1) * 512)
                        nc.vector.scalar_tensor_tensor(out=h[:, t, cols], in0=h[:, t, cols], scalar=mv[:, t, 0:1],
                                                       in1=grow[:, cols], op0=ALU.subtract, op1=ALU.mult
                                                       ).then_inc(scaled, 1)
                    dve.wait_ge(rstd_ready, k + 1)
                    for a in range(2):
                        cols = slice(a * 512, (a + 1) * 512)
                        dve.wait_ge(scaled, 2 * k + a + 1)
                        nc.vector.scalar_tensor_tensor(out=h[:, t, cols], in0=h[:, t, cols],
                                                       scalar=rstd[:, t:t + 1], in1=brow[:, cols], op0=ALU.mult,
                                                       op1=ALU.add).then_inc(norm_ready, 1)
                if last:
                    return
                for a in range(2):
                    dve.wait_ge(hThi_ready, 4 + 2 * n + a + 1)
                    nc.vector.tensor_tensor(hTlo[:, 4 * a:4 * a + 4, P:S], tr_bank(n, 1, a),
                                            hThi[:, 4 * a:4 * a + 4, P:S].bitcast(F32), ALU.subtract
                                            ).then_inc(hTlo_ready, 1)
                split_lo(NORM_CHUNK[n] + AHEAD)

            split_lo_half(0, 0)
            for b in range(4):
                dve.wait_ge(hThi_ready, b + 1)
                nc.vector.tensor_tensor(hTlo[:, 2 * b:2 * b + 2], hT[:, 2 * b:2 * b + 2],
                                        hThi[:, 2 * b:2 * b + 2].bitcast(F32), ALU.subtract).then_inc(hTlo_ready, 1)
            split_lo_half(0, 1)
            for c in range(1, AHEAD):
                split_lo(c)
            dve.wait_ge(widx_ready, 1)
            cols = (slice(0, P), slice(P, TRI))
            for i in range(I_HEADS):
                dve.wait_ge(relu_done, i + 1)
                for t in range(2):
                    w = wq_i[:, t, i:i + 1]
                    if i == 0:
                        op = nc.vector.tensor_scalar(idx[:, cols[t]], scratch[:, i, cols[t]], w, None, ALU.mult)
                    else:
                        dve.wait_ge(idx_step, 2 * i - 1 + t)
                        op = nc.vector.scalar_tensor_tensor(out=idx[:, cols[t]], in0=scratch[:, i, cols[t]],
                                                            scalar=w, in1=idx[:, cols[t]], op0=ALU.mult,
                                                            op1=ALU.add)
                    op.then_inc(idx_step, 1)
            split_lo(4)
            dve.wait_ge(crstd_ready, 1)
            dve.wait_ge(par_loaded, 48)
            for t in range(2):
                nc.vector.scalar_tensor_tensor(out=cn[:, t], in0=craw[:, t], scalar=rstd[:, t:t + 1], in1=kvrow[:],
                                               op0=ALU.mult, op1=ALU.mult).then_inc(c_ready, 1)
            dve.wait_ge(idx_masked, 1)
            done = 0
            for r in range(TOPK // 8):
                for t in range(2):
                    if r:
                        dve.wait_ge(topk_step, 4 * r - 1 + t)
                    nc.vector.max(m8[:, t], idx[:, cols[t]]).then_inc(topk_step, 1)
                for t in range(2):
                    dve.wait_ge(topk_step, 4 * r + 1 + t)
                    nc.vector.match_replace(idx[:, cols[t]], m8[:, t], idx[:, cols[t]], TAKEN
                                            ).then_inc(topk_step, 1)
                if r in (1, 3, 5):
                    split_lo(5 + r // 2)
            dve.wait_ge(topk_step, 4 * (TOPK // 8))
            nc.vector.tensor_scalar(dsel[:], idx, TAKEN / 1.5, MASKED, ALU.is_gt, ALU.mult).then_inc(dsel_ready, 1)
            dve.wait_ge(dsel_ready, 1)
            nc.vector.tensor_tensor(dsel[:], dsel[:], dcaus, ALU.add).then_inc(dsel_ready, 1)
            dve.wait_ge(dsel_ready, 2)

            for u in range(A_UNITS):
                if 0 <= u - 1 < A_HEADS:
                    logits(u - 1, 2.0 ** (-8.0 * u / A_HEADS), dsel[:])
                if A_FILL.get(u, (0, 0))[1] == 1:
                    split_lo(A_FILL[u][0] + AHEAD)
                if u in (7, 11):
                    normalise(u // 8, u // 8, GH * (u // 8 + 1))
                if u == 9:
                    evac_oT_lo(0, 0)

            for m in range(B_UNITS):
                if m < B_HEADS:
                    e = scratch[:, m % 2, :]
                    dve.wait_ge(l_ready, m + 1)
                    if m >= 3:
                        dve.wait_ge(rem_done, m - 2)
                    nc.vector.scalar_tensor_tensor(out=scratch[:, 2 + m % 3, :], in0=bank[m % 2][:, 0:TRI],
                                                   scalar=0.0, in1=e, op0=ALU.max, op1=ALU.add
                                                   ).then_inc(sp_ready, 1)
                if B_FILL[m][1] == 1:
                    split_lo(B_FILL[m][0] + AHEAD)
                if m == 1:
                    evac_oT_lo(1, 2)
                if m == 6:
                    evac_oT_lo(2, 4)
            evac_oT_lo(3, 6)

            def ffn_rows(L, base):
                split_lo(base + 4)
                for t in range(2):
                    n = FT * L + t
                    dve.wait_ge(silu_ready, n + 1)
                    if L:
                        dve.wait_ge(alo_ready, n - 1)
                    nc.vector.tensor_tensor(aful[:, t].rearrange("p (t f) -> p t f", t=2),
                                            sgate[:, t].rearrange("p (t f) -> p t f", t=2),
                                            rows_bank(t)[:, :, P:S], ALU.mult).then_inc(amul_ready, 1)
                for t in range(2):
                    dve.wait_ge(ahi_ready, FT * L + t + 1)
                    nc.vector.tensor_tensor(alo[:, t, :], bank[2 * t + 1][:, 0:S], ahi[:, t, :].bitcast(F32),
                                            ALU.subtract).then_inc(alo_ready, 1)
                split_lo(base + 5)

            def ffn_tile(L, c, t, i=0, more=1, alo_first=False):
                n = FT * L + t + 4 * i
                dve.wait_ge(silu_ready, n + 1)
                dve.wait_ge(chunk_used, c + 1 + RING * i)
                dve.wait_ge(alo_ready, n - 1)
                nc.vector.tensor_tensor(aful[:, t % 2], sgate[:, t % 2], bank[2 * (t % 2) + 1][:, 0:S], ALU.mult
                                        ).then_inc(amul_ready, 1)
                if more and not alo_first:
                    split_lo(c + AHEAD, i)
                dve.wait_ge(ahi_ready, n + 1)
                nc.vector.tensor_tensor(alo[:, FF_SLOT[t], :], aful[:, t % 2], ahi[:, FF_SLOT[t], :].bitcast(F32),
                                        ALU.subtract).then_inc(alo_ready, 1)
                if more and alo_first:
                    split_lo(c + AHEAD, i)

            def ffn(L):
                base = L0_FFN if L == 0 else L1_FFN
                ffn_rows(L, base)
                for t in (2, 3):
                    ffn_tile(L, base + t, t)
                with dve.Fori(0, LOOPS) as i:
                    for j in range(2):
                        c = base + 4 + 3 * j
                        split_lo(c + AHEAD, i)
                        ffn_tile(L, c + 1, 4 + 2 * j, i)
                        ffn_tile(L, c + 2, 5 + 2 * j, i)
                c = base + 4 + RING * LOOPS
                for at in range(4):
                    more = c + at + AHEAD < CHUNKS
                    if at < 2:
                        ffn_tile(L, c + at, 4 + 4 * LOOPS + at, 0, more, at == 1)
                    elif more:
                        split_lo(c + at + AHEAD)

            norm(0)
            ffn(0)
            norm(1)

            for q in range(3):
                split_lo(L1_IN + q + AHEAD)
            for u in range(C_UNITS):
                if u in C_AT:
                    hd = C_AT[u]
                    logits(A_HEADS + hd, 2.0 ** (-8.0 * (hd + 1) / C_HEADS), dcaus)
                if u in C_NORM:
                    g = C_NORM[u]
                    normalise(4 + g, 2 + g, A_HEADS + B_HEADS + GH * (g + 1))
                if u in C_FILL and C_FILL[u][1] == 1:
                    split_lo(L1_IN + C_FILL[u][0] + AHEAD)
                if u in C_TURN:
                    evac_oT_lo(4 + C_TURN[u], 2 * C_TURN[u])
            norm(2)
            ffn(1)
            norm(3)

        @block.tensor
        def _(pe):
            mm = nc.tensor.matmul
            HT_PASSES = ((whi, hThi), (whi, hTlo), (wlo, hThi))
            AT_PASSES = ((whi, ahi), (whi, alo), (wlo, ahi))

            def chunk(c, i=0):
                pe.wait_ge(wlo_ready, 2 * c + 2 + 2 * RING * i)

            def cols_out(dst, slot, off, first=False):
                for k in range(KT):
                    if first and k % 2 == 0:
                        pe.wait_ge(hTlo_ready, k // 2 + 1)
                    for j, (w, a) in enumerate(HT_PASSES):
                        last = mm(dst, w[:, slot, off + k * P:off + (k + 1) * P], a[:, k, :],
                                  start=(k == 0 and j == 0), stop=(k == KT - 1 and j == 2))
                return last

            def rows_out(dst, slot, t, n=0):
                for k in range(KT):
                    if n and t == 0 and k % 2 == 0:
                        pe.wait_ge(hTlo0_ready, 4 * (n - 1) + k // 2 + 1)
                    if n and t == 1 and k % 4 == 0:
                        pe.wait_ge(hTlo_ready, 4 + 2 * (n - 1) + k // 4 + 1)
                    for j, (w, a) in enumerate(HT_PASSES):
                        last = mm(dst, a[:, k, t * P:(t + 1) * P], w[:, slot, k * S:(k + 1) * S],
                                  start=(k == 0 and j == 0), stop=(k == KT - 1 and j == 2))
                return last

            def proj_half(c, n, half, is_v):
                if half == 0:
                    chunk(c)
                    if n >= 2:
                        pe.wait_ge(proj_evac, n - 1)
                dst = bank[4 + n % 2][:, half * S:(half + 1) * S]
                if is_v:
                    last = rows_out(dst, c % RING, half)
                else:
                    last = cols_out(dst, c % RING, half * KT * P)
                if half == 1:
                    last.then_inc(chunk_used, 1)

            def out_part(c, kts, t, a, start=False, stop=False):
                for j in range(2):
                    for q, (w, o) in enumerate(AT_PASSES):
                        last = mm(bank[4 + 2 * t + a][:], o[:, kts[j], t * P:(t + 1) * P],
                                  w[:, c % RING, j * D + a * 512:j * D + (a + 1) * 512],
                                  start=(start and q == 0 and j == 0), stop=(stop and q == 2 and j == 1),
                                  skip_group_check=True)
                return last

            def out_chunk(c, kts, start=False):
                for t in range(2):
                    for a in range(2):
                        last = out_part(c, kts, t, a, start)
                last.then_inc(chunk_used, 1)

            def last_out(parts, n, before_end=None, rest=None):
                for c, kts, alos in parts:
                    chunk(c)
                    if alos:
                        pe.wait_ge(alo_ready, alos)
                    end = c == parts[-1][0]
                    for a in range(2):
                        last = out_part(c, kts, 0, a, stop=end)
                        if end:
                            last.then_inc(acc_done, 1)
                for a in range(2):
                    if a == 1 and rest:
                        out_part(rest, (4, 5), 1, 1).then_inc(chunk_used, 1)
                    for c, kts, _ in parts:
                        if a == 1 and before_end and c == parts[-1][0]:
                            before_end()
                        last = out_part(c, kts, 1, a, stop=(c == parts[-1][0]))
                        if a == 1:
                            last.then_inc(chunk_used, 1)
                    if a == 0:
                        last.then_inc(acc_done, 1)

            def transpose_group(G):
                pe.wait_ge(otok_ready, turned_groups(G))
                for k in range(2):
                    for t in range(2):
                        last = nc.tensor.transpose(bank[2 + G % 2][:, k * S + t * P:k * S + (t + 1) * P],
                                                   otok[:, G % 2, t * S + k * P:t * S + (k + 1) * P], ident)
                last.then_inc(otr_done, 1)

            def transpose_probs(n):
                pe.wait_ge(probs_ready, n + 1)
                if n >= 1:
                    pe.wait_ge(probT_ready, n)
                for b in range(3):
                    last = nc.tensor.transpose(bank[1][:, b * P:(b + 1) * P], prob[:, n % 3, b * P:(b + 1) * P],
                                               ident)
                last.then_inc(probT_done, 1)

            def free_group_bank(G):
                if G >= 2:
                    pe.wait_ge(oTlo_ready, G - 1)

            def dots(i):
                p = DH * (i % 2)
                for t in range(2):
                    last = mm(bank[i][:, t * P:t * P + (t + 1) * P], kT[p:p + DH, 6 + i // 2, t * P:(t + 1) * P],
                              kiT[p:p + DH, 0:(t + 1) * P], start=True, stop=True)
                last.then_inc(dots_done, 1)

            pe.wait_ge(wlo_ready, 1)
            cols_out(bank[4][:, 0:S], 0, 0, True)
            chunk(0)
            cols_out(bank[4][:, S:2 * S], 0, KT * P).then_inc(chunk_used, 1)
            for half in range(2):
                proj_half(1, 1, half, False)
            pe.wait_ge(proj_evac, 1)
            pe.wait_ge(dist_loaded, 16)
            for t in range(2):
                last = nc.tensor.transpose(craw[:, t], crawT[:, t * P:(t + 1) * P], ident)
            last.then_inc(craw_done, 1)
            for t in range(2):
                last = nc.tensor.transpose(bank[6][:, t * I_HEADS:(t + 1) * I_HEADS], wT[:, t * P:(t + 1) * P],
                                           ident[DH:DH + I_HEADS, DH:DH + I_HEADS])
            last.then_inc(widx_done, 1)
            pe.wait_ge(proj_evac, 2)
            for i in range(I_HEADS):
                dots(i)
            for c in (2, 3):
                for half in range(2):
                    proj_half(c, c, half, False)
            pe.wait_ge(c_ready, 2)
            pe.wait_ge(widx_ready, 1)
            for t in range(2):
                last = nc.tensor.transpose(bank[6][:, t * P:(t + 1) * P], cn[:, t], ident)
            last.then_inc(ctr_done, 1)

            def out_half(c, q, half, groups, evacs):
                kts = (2 * q, 2 * q + 1)
                if half == 0:
                    chunk(c)
                    pe.wait_ge(oTlo_ready, groups + q + 1)
                    if q == 0:
                        pe.wait_ge(proj_evac, evacs)
                for a in range(1 if q == 2 and half == 1 else 2):
                    last = out_part(c, kts, half, a, q == 0)
                if half == 1 and q < 2:
                    last.then_inc(chunk_used, 1)

            def fill_l0(fill):
                if fill is None:
                    return
                c, half = fill
                if c < L0_OUT:
                    proj_half(c, c, half, (c - 4) % 3 == 2)
                else:
                    out_half(c, c - L0_OUT, half, 0, L0_OUT)

            pe.wait_ge(relu_done, I_HEADS)
            for u in range(A_UNITS):
                fill_l0(A_FILL.get(u))
                if 0 <= u - 4 < A_HEADS:
                    hd = u - 4
                    pe.wait_ge(olat_ready, hd + 1)
                    if hd % GH == 0:
                        free_group_bank(hd // GH)
                    for t in range(2):
                        at = t * S + (hd % GH) * DH
                        last = mm(bank[2 + hd // GH][:, at:at + DH], olT[:, t * P:(t + 1) * P],
                                  ukv[:, 1].rearrange("p a b -> p (a b)")[:, hd * DH:(hd + 1) * DH], start=True,
                                  stop=True)
                    last.then_inc(pv_done, 1)
                if 0 <= u - 3 < A_HEADS:
                    n = u - 3
                    pe.wait_ge(probT_ready, n + 1)
                    if n >= 1:
                        pe.wait_ge(olat_ready, n)
                    mm(bank[7][:, 0:P], cn[:, 0], probT[:, n % 2, 0:P], start=True, stop=True)
                    mm(bank[7][:, P:S], cn[:, 0], probT[:, n % 2, P:S], start=True, stop=False)
                    mm(bank[7][:, P:S], cn[:, 1], probT[:, n % 2, S:TRI], start=False, stop=True
                       ).then_inc(olat_done, 1)
                if 0 <= u - 2 < A_HEADS:
                    transpose_probs(u - 2)
                if 0 <= u - 1 < A_HEADS:
                    n = u - 1
                    pe.wait_ge(qlat_ready, n + 1)
                    pe.wait_ge(cT_ready, 1)
                    if n >= 1:
                        pe.wait_ge(logits_done, n)
                    for t in range(2):
                        last = mm(bank[0][:, t * P:t * P + (t + 1) * P], qlT[:, t * P:(t + 1) * P],
                                  cT[:, 0:(t + 1) * P], start=True, stop=True)
                    last.then_inc(scores_done, 1)
                if u < A_HEADS:
                    p = DH * (u % 2)
                    if u == 0:
                        pe.wait_ge(proj_evac, 4)
                        pe.wait_ge(cT_ready, 1)
                    else:
                        pe.wait_ge(qlat_ready, u)
                    mm(bank[6][:, 0:S], ukv[p:p + DH, 0].rearrange("p a b -> p (a b)")[:, (u // 2) * P:(u // 2 + 1) * P],
                       qT[p:p + DH, 4 + u // 2, :], start=True, stop=True).then_inc(qlat_done, 1)
                if u == 9:
                    transpose_group(0)

            for m in range(B_UNITS):
                if m < B_HEADS:
                    pe.wait_ge(proj_evac, 6 + 3 * (m // GH))
                    if m >= 2:
                        pe.wait_ge(a_exp, m - 1)
                    p, jt, z = DH * (m % 2), m // 2, bank[m % 2]
                    mm(z[:, 0:S], kT[p:p + DH, jt, 0:P], qT[p:p + DH, jt, :], start=True, stop=False,
                       skip_group_check=True)
                    mm(z[:, S:TRI], kT[p:p + DH, jt, P:S], qT[p:p + DH, jt, P:S], start=False, stop=False,
                       skip_group_check=True).then_inc(z_done, 1)
                if 0 <= m - 2 < B_HEADS:
                    n = m - 2
                    G = 2 + n // GH
                    if n % GH == 0:
                        free_group_bank(G)
                        pe.wait_ge(proj_evac, 7 + 3 * (n // GH))
                    pe.wait_ge(a_masked, n + 1)
                    a = prob[:, n % 3, :]
                    vh = slice(n * DH, (n + 1) * DH)
                    o = bank[2 + G % 2][DH * (n % 2):DH * (n % 2) + DH, (n % GH) // 2 * S:((n % GH) // 2 + 1) * S]
                    mm(o, v[:, 0, vh], a[:, 0:S], start=True, stop=False)
                    mm(o[:, P:S], v[:, 1, vh], a[:, S:TRI], start=False, stop=True).then_inc(pv_done, 1)
                if 0 <= m - 1 < B_HEADS:
                    n = m - 1
                    sp_t = scratch[:, 2 + n % 3, :]
                    z = bank[n % 2]
                    pe.wait_ge(sp_masked, n + 1)
                    mm(z[:, 0:S], negtri, sp_t[:, 0:S], start=False, stop=False, skip_group_check=True)
                    mm(z[:, P:S], negones, sp_t[:, S:TRI], start=False, stop=False, skip_group_check=True)
                    mm(z[:, S:TRI], negtri, sp_t[:, S:TRI], start=False, stop=True, skip_group_check=True
                       ).then_inc(rem_done, 1)
                fill_l0(B_FILL[m])
                if m == 1:
                    transpose_group(1)
            pe.wait_ge(oTlo_ready, 4)
            last_out(((L0_OUT + 3, (6, 7), 0),), 0, rest=L0_OUT + 2)

            def norm_transposes(n, t):
                for k in range(KT):
                    if k % 4 == 0:
                        pe.wait_ge(norm_ready, 4 * n + 2 * t + k // 4 + 1)
                    last = nc.tensor.transpose(bank[TR_BANK[n] + 2 * t + k // 4][:, (k % 4) * P:(k % 4 + 1) * P],
                                               h[:, t, k * P:(k + 1) * P], ident)
                    if k % 4 == 3:
                        last.then_inc(tr1_done if t else tr0_done, 1)

            def gate_up_rows(L, c, tile, t):
                if t == 0:
                    chunk(c)
                last = rows_out(rows_bank(tile)[:, t], c % RING, t, 2 * L + 1)
                if t == 1:
                    last.then_inc(chunk_used, 1)

            def turn_rows(L, tile):
                pe.wait_ge(amul_ready, FT * L + tile + 1)
                for t in range(2):
                    last = nc.tensor.transpose(bank[2 * tile + 1][:, t * P:(t + 1) * P],
                                               aful[:, tile, t * P:(t + 1) * P], ident)
                last.then_inc(ff_turned, 1)

            def gate_up(L, c, t, i=0):
                n = FT * L + t + 4 * i
                chunk(c, i)
                pe.wait_ge(alo_ready if t < 4 else amul_ready, n - 1)
                cols_out(bank[2 * (t % 2)][:, 0:S], c % RING, 0).then_inc(gate_done, 1)
                cols_out(bank[2 * (t % 2) + 1][:, 0:S], c % RING, KT * P).then_inc(chunk_used, 1)

            def down(L, c, p, i=0):
                chunk(c, i)
                pe.wait_ge(alo_ready, FT * L + 2 * p + 2 + 4 * i)
                out_chunk(c, (2 * p % 4, 2 * p % 4 + 1))

            def ffn(L, n):
                base = L0_FFN if L == 0 else L1_FFN
                norm_transposes(n, 0)
                gate_up_rows(L, base, 0, 0)
                norm_transposes(n, 1)
                gate_up_rows(L, base + 1, 1, 0)
                gate_up_rows(L, base, 0, 1)
                gate_up_rows(L, base + 1, 1, 1)
                turn_rows(L, 0)
                for b in range(4, 8):
                    mm(bank[b][:], zeros[:, 0:P], zeros[:], start=True, stop=False, skip_group_check=True)
                turn_rows(L, 1)
                for t in (2, 3):
                    gate_up(L, base + t, t)
                with pe.Fori(0, LOOPS) as i:
                    for j in range(2):
                        c = base + 4 + 3 * j
                        down(L, c, j, i)
                        gate_up(L, c + 1, 4 + 2 * j, i)
                        gate_up(L, c + 2, 5 + 2 * j, i)
                c, p = base + 4 + RING * LOOPS, 2 * LOOPS
                gate_up(L, c, 2 * p + 4)
                gate_up(L, c + 1, 2 * p + 5)
                last_out([(c + 2 + j, FF_SLOT[2 * (p + j):2 * (p + j) + 2], FT * L + 2 * (p + j) + 2)
                          for j in range(3)], n + 1, (lambda: norm_transposes(1, 0)) if L == 0 else None)

            ffn(0, 0)

            chunk(L1_IN)
            pe.wait_ge(proj_evac, 9)
            rows_out(bank[4][:, 0:S], L1_IN % RING, 0, 2)
            norm_transposes(1, 1)
            rows_out(bank[4][:, S:2 * S], L1_IN % RING, 1, 2).then_inc(chunk_used, 1)
            for q in (1, 2):
                for half in range(2):
                    proj_half(L1_IN + q, 10 + q, half, False)
            for u in range(C_UNITS):
                if u in C_TURN and C_TURN[u] == 3:
                    transpose_group(7)
                if u in C_FILL:
                    q, half = C_FILL[u]
                    if q < 12:
                        proj_half(L1_IN + q, 10 + q, half, q % 3 == 2)
                    else:
                        out_half(L1_IN + q, q - 12, half, 4, 22)
                if u - 3 in C_AT:
                    hd = C_AT[u - 3]
                    n = A_HEADS + hd
                    G = 4 + hd // GH
                    if hd % GH == 0:
                        free_group_bank(G)
                        pe.wait_ge(proj_evac, 10 + 3 * (hd // GH) + 3)
                    pe.wait_ge(probT_ready, n + 1)
                    pt = probT[:, n % 2]
                    vh = slice(hd * DH, (hd + 1) * DH)
                    o = bank[2 + G % 2]
                    at = (hd % GH) * DH
                    mm(o[:, at:at + DH], pt[:, 0:P], v[:, 0, vh], start=True, stop=True)
                    mm(o[:, S + at:S + at + DH], pt[:, P:S], v[:, 0, vh], start=True, stop=False)
                    mm(o[:, S + at:S + at + DH], pt[:, S:TRI], v[:, 1, vh], start=False, stop=True
                       ).then_inc(pv_done, 1)
                if u - 2 in C_AT:
                    transpose_probs(A_HEADS + C_AT[u - 2])
                if u in C_AT:
                    hd = C_AT[u]
                    n = A_HEADS + hd
                    pe.wait_ge(proj_evac, 10 + 3 * (hd // GH) + (2 if hd >= GH else 3))
                    pe.wait_ge(logits_done, n)
                    p = DH * (hd % 2)
                    for t in range(2):
                        last = mm(bank[0][:, t * P:t * P + (t + 1) * P], qT[p:p + DH, hd // 2, t * P:(t + 1) * P],
                                  kT[p:p + DH, hd // 2, 0:(t + 1) * P], start=True, stop=True)
                    last.then_inc(scores_done, 1)
                if u in C_TURN and C_TURN[u] < 3:
                    transpose_group(4 + C_TURN[u])
            pe.wait_ge(oTlo_ready, 8)
            last_out(((L1_OUT + 3, (6, 7), 0),), 2, rest=L1_OUT + 2)
            ffn(1, 2)


def _blocks(w, cols):
    return w[:, cols].reshape(KT, P, -1).transpose(1, 0, 2)


def _tiles(w, start, n):
    import numpy as np
    return np.stack([_blocks(w, slice(start + P * j, start + P * (j + 1))) for j in range(n)], 1)


def _rows(w, kt):
    return w[kt * P:(kt + 2) * P].reshape(2, P, -1).transpose(1, 0, 2)


def weight_stream(w_in0, w_out0, w_in1, w_out1, gate, up, down):
    import numpy as np
    ckv, qi, ki, qb = 512, 640, 896, 964
    kb, vb = qb + 512, qb + 1024
    chunks = []

    def add(*parts):
        chunks.append(np.concatenate([p.reshape(P, -1) for p in parts], 1))

    keys = np.concatenate([w_in0[:, ki:ki + DH + I_HEADS], w_in0[:, ki:ki + DH - I_HEADS]], 1)
    add(_tiles(keys, 0, 1), _blocks(w_in0, slice(ckv, ckv + P)))
    add(_tiles(w_in0, qi, 2))
    add(_tiles(w_in0, 0, 2))
    add(_tiles(w_in0, 256, 2))
    for g in range(2):
        add(_tiles(w_in0, qb + S * g, 2))
        add(_tiles(w_in0, kb + S * g, 2))
        add(_blocks(w_in0, slice(vb + S * g, vb + S * (g + 1))))

    def out_rows(w):
        for q in range(4):
            add(_rows(w, 2 * q))

    def ffn(L):
        def gu(t):
            add(_tiles(gate[L], t * P, 1), _tiles(up[L], t * P, 1))
        for t in range(2):
            cols = slice(t * P, (t + 1) * P)
            add(np.concatenate([_blocks(gate[L], cols), _blocks(up[L], cols)], 2))
        for p in range(1, PAIRS):
            gu(2 * p)
            gu(2 * p + 1)
            if p < PAIRS - 2:
                add(_rows(down[L], 2 * (p - 1)))
        for p in range(PAIRS - 3, PAIRS):
            add(_rows(down[L], 2 * p))

    out_rows(w_out0)
    ffn(0)
    for g in range(4):
        if g == 0:
            add(_blocks(w_in1, slice(2 * D, 2 * D + S)))
        add(_tiles(w_in1, S * g, 2))
        add(_tiles(w_in1, D + S * g, 2))
        if g > 0:
            add(_blocks(w_in1, slice(2 * D + S * g, 2 * D + S * (g + 1))))
    out_rows(w_out1)
    ffn(1)
    return np.stack(chunks)


def constants():
    import numpy as np
    q = np.arange(P)[:, None]
    k = np.arange(P)[None, :]
    near = np.where(k <= q, k - q, MASKED)
    far = k - (q + P)
    tri = np.where(q >= k, -1.0, 0.0)
    return np.concatenate([near, far, near, tri, -np.ones((P, P)), np.eye(P)], 1).astype(np.float32)


def kernel(**inputs):
    import numpy as np
    import concourse.bacc as bacc
    from concourse.bass_utils import run_bass_kernel_spmd

    a = {k: np.asarray(w) for k, w in inputs.items()}
    xx = a["x"][0]
    w0 = a["even_w_in"][0]
    arrays = {
        "x_in": xx.reshape(2, P, D).transpose(1, 0, 2),
        "xT_in": xx.T.reshape(KT, P, S).transpose(1, 0, 2),
        "stream_in": weight_stream(w0, a["even_w_out"][0], a["odd_w_in"][0], a["odd_w_out"][0], a["ffn_gate"],
                                   a["ffn_up"], a["ffn_down"]),
        "w_uk_in": a["even_w_uk"][0].reshape(4, 2, DH, P).transpose(1, 2, 0, 3).reshape(P, 4 * P),
        "w_uv_in": a["even_w_uv"][0].transpose(1, 0, 2).reshape(P, A_HEADS * DH),
        "kv_norm_in": a["even_kv_norm"][0],
        "ln_rows_in": np.stack([np.stack([a[f"ln_{w}_g"][L], a[f"ln_{w}_b"][L]]) for L in range(2)
                                for w in ("mix", "ffn")]),
        "consts_in": constants(),
    }
    nc = bacc.Bacc("TRN2", target_bir_lowering=False, num_devices=1)
    ap = {}
    for k in arrays:
        arrays[k] = np.ascontiguousarray(arrays[k])
        ap[k] = nc.dram_tensor(k, arrays[k].shape, mybir.dt.from_np(arrays[k].dtype), kind="ExternalInput").ap()
    out = nc.dram_tensor("out_0", (2, P, D), F32, kind="ExternalOutput").ap()
    build(nc, ap["x_in"], ap["xT_in"], ap["stream_in"],
          ap["w_uk_in"].rearrange("p (a b) -> p a b", a=4), ap["w_uv_in"].rearrange("p (a b) -> p a b", a=4),
          ap["kv_norm_in"], ap["ln_rows_in"], ap["consts_in"], out)
    r = run_bass_kernel_spmd(nc, [arrays], core_ids=[0])
    return r.results[0]["out_0"].reshape(1, S, D)
```
